# Optimizing a Trainium2 kernel written in Bass

```python
import jax, jax.numpy as jnp
from jax import lax
import numpy as np

D_MODEL = 1024
BATCH = 1
SEQ = 1024
DEPTH = 1

PLE_DIM = 256
D_MIX = D_MODEL
GDN_HEADS = 4
GDN_DK = 128
GDN_DV = 128
GDN_QK_W = GDN_HEADS * GDN_DK
GDN_V_W = GDN_HEADS * GDN_DV
GDN_CONV = 4
GDN_CHUNK = 64
CONF_CH = D_MIX - GDN_V_W
CONF_WIDTH = 31
N_GROUPS = 8
EXPERTS_PER_GROUP = 8
N_EXPERTS = N_GROUPS * EXPERTS_PER_GROUP
TOP_K = 2
D_EXPERT = 256
MOE_BLOCK = 128
EPS = 1e-6
IN_COLS = 2 * GDN_QK_W + 2 * GDN_V_W + 2 * GDN_HEADS + 2 * CONF_CH

kernel_name = 'hybrid_gdn_conformer_hmoe_block'

def _rmsnorm(x, g):
    xf = x.astype(jnp.float32)
    y = xf * lax.rsqrt(jnp.mean(xf * xf, axis=-1, keepdims=True) + EPS)
    return (y * g.astype(jnp.float32)).astype(x.dtype)

def _layernorm(x, g, b):
    xf = x.astype(jnp.float32)
    mu = jnp.mean(xf, axis=-1, keepdims=True)
    var = jnp.mean(jnp.square(xf - mu), axis=-1, keepdims=True)
    y = (xf - mu) * lax.rsqrt(var + EPS)
    return (y * g.astype(jnp.float32) + b.astype(jnp.float32)).astype(x.dtype)

def _l2norm(x):
    return x * lax.rsqrt(jnp.sum(x * x, axis=-1, keepdims=True) + EPS)

def _causal_depthwise_conv(x, w):
    K, C = w.shape
    return lax.conv_general_dilated(
        x, w[:, None, :].astype(x.dtype), window_strides=(1,), padding=[(K - 1, 0)],
        dimension_numbers=('NWC', 'WIO', 'NWC'), feature_group_count=C)

def _gated_delta_rule_chunked(q, k, v, g, beta):
    B, T, H, DK = q.shape
    DV = v.shape[-1]
    C = GDN_CHUNK
    NC = T // C

    def chunks(t):
        return jnp.moveaxis(t.reshape((B, NC, C, H) + t.shape[3:]), 3, 1)

    q, k, v, g, beta = chunks(q), chunks(k), chunks(v), chunks(g), chunks(beta)
    gc = jnp.cumsum(g, axis=-1)
    causal = jnp.tril(jnp.ones((C, C), dtype=bool))
    strict = jnp.tril(jnp.ones((C, C), dtype=bool), -1)
    decay = jnp.exp(jnp.where(causal, gc[..., :, None] - gc[..., None, :], -jnp.inf))
    k_beta = k * beta[..., None]
    v_beta = v * beta[..., None]
    L = jnp.where(strict, jnp.einsum('bhncd,bhnsd->bhncs', k_beta, k) * decay, 0.0)
    eye = jnp.broadcast_to(jnp.eye(C, dtype=L.dtype), L.shape)
    Tm = lax.linalg.triangular_solve(L + eye, eye, left_side=True, lower=True, unit_diagonal=True)
    u = jnp.einsum('bhncs,bhnse->bhnce', Tm, v_beta)
    w = jnp.einsum('bhncs,bhnsd->bhncd', Tm, k_beta * jnp.exp(gc)[..., None])
    qk = jnp.einsum('bhncd,bhnsd->bhncs', q, k) * decay
    q_dec = q * jnp.exp(gc)[..., None]
    k_dec = k * jnp.exp(gc[..., -1:] - gc)[..., None]
    g_tot = jnp.exp(gc[..., -1])
    xs = tuple(jnp.moveaxis(t, 2, 0) for t in (u, w, qk, q_dec, k_dec, g_tot))

    def step(S, xs_n):
        u_n, w_n, qk_n, qd_n, kd_n, gt_n = xs_n
        v_new = u_n - jnp.einsum('bhcd,bhde->bhce', w_n, S)
        o_n = jnp.einsum('bhcd,bhde->bhce', qd_n, S) + jnp.einsum('bhcs,bhse->bhce', qk_n, v_new)
        S = S * gt_n[..., None, None] + jnp.einsum('bhcd,bhce->bhde', kd_n, v_new)
        return S, o_n

    S0 = jnp.zeros((B, H, DK, DV), jnp.float32)
    _, o = lax.scan(step, S0, xs)
    return o.transpose(1, 0, 3, 2, 4).reshape(B, T, H, DV)

def _mixers(n1, w_in, w_conv_qkv, a_log, dt_bias, g_gdn_out, b_glu, w_conv_dw, b_conv_dw,
            ln_conv_g, ln_conv_b):
    B, T, _ = n1.shape
    proj = n1 @ w_in
    o1 = 2 * GDN_QK_W + GDN_V_W
    o2 = o1 + GDN_V_W
    o3 = o2 + GDN_HEADS
    o4 = o3 + GDN_HEADS
    qkv, z, b_raw, a_raw, glu_in = jnp.split(proj, [o1, o2, o3, o4], axis=-1)

    qkv = jax.nn.silu(_causal_depthwise_conv(qkv, w_conv_qkv)).astype(jnp.float32)
    q, k, v = jnp.split(qkv, [GDN_QK_W, 2 * GDN_QK_W], axis=-1)
    q = _l2norm(q.reshape(B, T, GDN_HEADS, GDN_DK)) * (GDN_DK ** -0.5)
    k = _l2norm(k.reshape(B, T, GDN_HEADS, GDN_DK))
    v = v.reshape(B, T, GDN_HEADS, GDN_DV)
    beta = jax.nn.sigmoid(b_raw.astype(jnp.float32))
    g = -jnp.exp(a_log.astype(jnp.float32)) * jax.nn.softplus(
        a_raw.astype(jnp.float32) + dt_bias.astype(jnp.float32))
    o = _gated_delta_rule_chunked(q, k, v, g, beta)
    o = (o * lax.rsqrt(jnp.mean(o * o, axis=-1, keepdims=True) + EPS) * g_gdn_out.astype(jnp.float32)
         * jax.nn.silu(z.astype(jnp.float32).reshape(B, T, GDN_HEADS, GDN_DV)))
    y_gdn = o.reshape(B, T, GDN_V_W).astype(n1.dtype)

    u = glu_in + b_glu
    u = u[..., :CONF_CH] * jax.nn.sigmoid(u[..., CONF_CH:])
    c = _causal_depthwise_conv(u, w_conv_dw) + b_conv_dw
    y_conv = jax.nn.silu(_layernorm(c, ln_conv_g, ln_conv_b))

    return jnp.concatenate([y_gdn, y_conv], axis=-1)

def _hierarchical_moe(xn, w_group_router, w_expert_router, w_up, w_down):
    B, T, D = xn.shape
    N = B * T
    xf = xn.reshape(N, D)
    group_p = jax.nn.softmax((xf @ w_group_router).astype(jnp.float32), axis=-1)
    g_w, g_idx = lax.top_k(group_p, 1)
    e_logits = (xf @ w_expert_router).astype(jnp.float32).reshape(N, N_GROUPS, EXPERTS_PER_GROUP)
    in_group = jnp.take_along_axis(e_logits, g_idx[:, :, None], axis=1)[:, 0]
    e_w, e_idx = lax.top_k(jax.nn.softmax(in_group, axis=-1), TOP_K)
    gate = g_w * (e_w / jnp.sum(e_w, axis=-1, keepdims=True))
    expert = g_idx * EXPERTS_PER_GROUP + e_idx

    NK = N * TOP_K
    flat_e = expert.reshape(-1)
    flat_tok = jnp.repeat(jnp.arange(N, dtype=jnp.int32), TOP_K)
    flat_w = gate.reshape(-1)
    order = jnp.argsort(flat_e)
    se, st, sw = flat_e[order], flat_tok[order], flat_w[order]
    counts = jnp.bincount(flat_e, length=N_EXPERTS)
    starts = jnp.cumsum(counts) - counts
    padded = (counts + MOE_BLOCK - 1) // MOE_BLOCK * MOE_BLOCK
    pend = jnp.cumsum(padded)
    pstart = pend - padded
    pos = pstart[se] + jnp.arange(NK, dtype=jnp.int32) - starts[se]
    nb = -(-NK // MOE_BLOCK) + N_EXPERTS
    P = nb * MOE_BLOCK
    buf_tok = jnp.zeros((P,), jnp.int32).at[pos].set(st)
    buf_w = jnp.zeros((P,), jnp.float32).at[pos].set(sw)
    block_expert = jnp.minimum(
        jnp.searchsorted(pend, jnp.arange(nb, dtype=jnp.int32) * MOE_BLOCK, side='right'), N_EXPERTS - 1)
    xb = xf[buf_tok].reshape(nb, MOE_BLOCK, D)

    def expert_block(args):
        x_blk, e = args
        a, b = jnp.split(x_blk @ w_up[e], 2, axis=-1)
        return (jax.nn.silu(a) * b) @ w_down[e]

    yb = lax.map(expert_block, (xb, block_expert)).reshape(P, D)
    y = jax.ops.segment_sum(yb * buf_w[:, None].astype(yb.dtype), buf_tok, num_segments=N)
    return y.reshape(B, T, D)

def setup_inputs(seed: int = 0) -> dict:
    key = jax.random.key(seed)
    ks = jax.random.split(key, 24)
    f32 = jnp.float32

    def nrm(k, shape, scale):
        return jax.random.normal(k, shape, f32) * scale

    def gain(k, shape):
        return 1.0 + 0.05 * jax.random.normal(k, shape, f32)

    dt = jnp.exp(jax.random.uniform(ks[5], (DEPTH, GDN_HEADS), f32, np.log(1e-3), np.log(1e-1)))
    return {
        'x': nrm(ks[0], (BATCH, SEQ, D_MODEL), 1.0),
        'p': nrm(ks[1], (DEPTH, BATCH, SEQ, PLE_DIM), 1.0),
        'g_mix': gain(ks[2], (DEPTH, D_MODEL)),
        'w_in': nrm(ks[3], (DEPTH, D_MODEL, IN_COLS), D_MODEL ** -0.5),
        'w_conv_qkv': nrm(ks[4], (DEPTH, GDN_CONV, 2 * GDN_QK_W + GDN_V_W), GDN_CONV ** -0.5),
        'a_log': jnp.log(jax.random.uniform(ks[6], (DEPTH, GDN_HEADS), f32, 1.0, 16.0)),
        'dt_bias': dt + jnp.log(-jnp.expm1(-dt)),
        'g_gdn_out': gain(ks[7], (DEPTH, GDN_DV)),
        'b_glu': nrm(ks[8], (DEPTH, 2 * CONF_CH), 0.02),
        'w_conv_dw': nrm(ks[9], (DEPTH, CONF_WIDTH, CONF_CH), CONF_WIDTH ** -0.5),
        'b_conv_dw': nrm(ks[10], (DEPTH, CONF_CH), 0.02),
        'ln_conv_g': gain(ks[11], (DEPTH, CONF_CH)),
        'ln_conv_b': nrm(ks[12], (DEPTH, CONF_CH), 0.02),
        'w_out': nrm(ks[13], (DEPTH, D_MIX, D_MODEL), D_MIX ** -0.5),
        'g_moe': gain(ks[14], (DEPTH, D_MODEL)),
        'w_group_router': nrm(ks[15], (DEPTH, D_MODEL, N_GROUPS), D_MODEL ** -0.5),
        'w_expert_router': nrm(ks[16], (DEPTH, D_MODEL, N_EXPERTS), D_MODEL ** -0.5),
        'w_up': nrm(ks[17], (DEPTH, N_EXPERTS, D_MODEL, 2 * D_EXPERT), D_MODEL ** -0.5),
        'w_down': nrm(ks[18], (DEPTH, N_EXPERTS, D_EXPERT, D_MODEL), D_EXPERT ** -0.5),
        'g_ple': gain(ks[19], (DEPTH, D_MODEL)),
        'w_ple_gate': nrm(ks[20], (DEPTH, D_MODEL, D_MODEL), D_MODEL ** -0.5),
        'w_ple_proj': nrm(ks[21], (DEPTH, PLE_DIM, D_MODEL), PLE_DIM ** -0.5),
        'g_final': gain(ks[22], (D_MODEL,)),
    }

def reference(x, p, g_mix, w_in, w_conv_qkv, a_log, dt_bias, g_gdn_out, b_glu, w_conv_dw,
              b_conv_dw, ln_conv_g, ln_conv_b, w_out, g_moe, w_group_router, w_expert_router,
              w_up, w_down, g_ple, w_ple_gate, w_ple_proj, g_final):
    h = x
    for i in range(DEPTH):
        n1 = _rmsnorm(h, g_mix[i])
        mix = _mixers(n1, w_in[i], w_conv_qkv[i], a_log[i], dt_bias[i], g_gdn_out[i], b_glu[i],
                      w_conv_dw[i], b_conv_dw[i], ln_conv_g[i], ln_conv_b[i])
        h = h + mix @ w_out[i]
        h = h + _hierarchical_moe(_rmsnorm(h, g_moe[i]), w_group_router[i], w_expert_router[i],
                                  w_up[i], w_down[i])
        ple_gate = jax.nn.sigmoid(_rmsnorm(h, g_ple[i]) @ w_ple_gate[i])
        h = h + ple_gate * (p[i] @ w_ple_proj[i])
    return _rmsnorm(h, g_final)


_drawn_inputs = setup_inputs


def setup_inputs(seed=0):
    import zlib

    import numpy as np

    out = dict(_drawn_inputs(seed))
    spreads = {}
    factors = {'b_glu': 3.714, 'ln_conv_b': 4.496, 'g_ple': 6.908}
    for name, (base, spread) in spreads.items():
        noise = np.random.default_rng([zlib.crc32(name.encode()), seed]).standard_normal(out[name].shape)
        drawn = base * np.exp(spread * noise) if base else spread * noise
        out[name] = __import__('jax').numpy.asarray(drawn.astype(out[name].dtype))
    for name, factor in factors.items():
        out[name] = (out[name] * factor).astype(out[name].dtype)
    return out
```

```python
from contextlib import ExitStack

import concourse.bass as bass
from concourse import mybir

P = 128
F32 = mybir.dt.float32
F32R = mybir.dt.float32r
F16 = mybir.dt.float16
BF16 = mybir.dt.bfloat16
I32 = mybir.dt.int32
ALU = mybir.AluOpType
ACT = mybir.ActivationFunctionType
AX = mybir.AxisListType
ds = bass.ds

EPS = 1e-6
NEG = -1.0e30


class Steps:

    def __init__(self, sem, names, credit=False):
        self.sem, self.names, self.next = sem, list(names), 0
        self.base = len(self.names) if credit else 0
        assert len(set(self.names)) == len(self.names)

    def __call__(self, name):
        assert self.names[self.next] == name, (self.names[self.next], name)
        self.next = (self.next + 1) % len(self.names)
        return self.sem, 1

    def give_credit(self, eng):
        eng.sem_inc(self.sem, self.base)

    def sem_at(self, name, i=0):
        return self.sem, self.base + i * len(self.names) + self.names.index(name) + 1


def hybrid_block_kernel(nc, x, p, g_mix, w_in, w_conv_qkv, a_log, dt_bias, g_gdn_out, b_glu,
                        w_conv_dw, b_conv_dw, ln_conv_g, ln_conv_b, w_out, g_moe, w_group_router,
                        w_expert_router, w_up, w_down, g_ple, w_ple_gate, w_ple_proj, g_final, out):
    T, D = x.shape[1], x.shape[2]
    NT, NJ = T // P, D // P
    H, DK = a_log.shape[1], g_gdn_out.shape[1]
    QKV = w_conv_qkv.shape[2]
    NQ = QKV // P
    KQ = w_conv_qkv.shape[1]
    KC, CF = w_conv_dw.shape[1], w_conv_dw.shape[2]
    NC_ = CF // P
    ZOFF = QKV
    BAOFF = ZOFF + H * DK
    GOFF = BAOFF + 2 * H
    CH = 64

    top = ExitStack()

    def sb(name, shape, dt=F32, ctx=None):
        return (ctx or top).enter_context(nc.sbuf_tensor(name, shape, dt))

    def psum(name, shape, dt=F32, ctx=None):
        return (ctx or top).enter_context(nc.psum_tensor(name, shape, dt))

    def sem(name):
        return top.enter_context(nc.semaphore(name))

    s_turn = sem("s_turn")

    def wait_alone(eng, sem_, value):
        eng.wait_ge(sem_, value)
        eng.sem_inc(s_turn, 1)

    def mm3(ps, lhs, rhs, first, last):
        for k, (a, b) in enumerate(((0, 0), (0, 1), (1, 0))):
            ins = nc.tensor.matmul(ps, lhs[a], rhs[b], start=first and k == 0, stop=last and k == 2)
        return ins

    with top:
        ident = sb("ident", [P, P])
        vecT = sb("vecT", [P, 2, P])
        gmix = sb("gmix", [P, NJ])
        ba = sb("ba", [P, NT, 2 * H])

        s_const = sem("s_const")
        s_loaded = sem("s_loaded")

        proj = ExitStack()
        convT = sb("convT", [P, NC_, T], ctx=proj)
        qkvT = sb("qkvT", [P, NQ, T], ctx=proj)
        zT = sb("zT", [P, H, T], ctx=proj)
        n1ctx = ExitStack()
        n1 = [sb("n1_hi", [P, NJ, T], F32R, n1ctx), sb("n1_lo", [P, NJ, T], F32R, n1ctx)]
        wraw = [sb(f"wraw{s}", [P, NJ, P], ctx=n1ctx) for s in range(2)]
        wh = [sb(f"wh{s}", [P, NJ, P], F32R, n1ctx) for s in range(2)]
        wl = [sb(f"wl{s}", [P, NJ, P], F32R, n1ctx) for s in range(2)]

        DW = lambda k, m: vecT[:, 0, ds(k * NC_ + m, 1)]
        CQ = lambda k, m: vecT[:, 1, ds(k * NQ + m, 1)]
        R0 = KQ * NQ
        BGLU = lambda m: vecT[:, 1, ds(R0 + m, 1)]
        BDW = lambda m: vecT[:, 1, ds(R0 + 2 * NC_ + m, 1)]
        LNG = lambda m: vecT[:, 1, ds(R0 + 3 * NC_ + m, 1)]
        LNB = lambda m: vecT[:, 1, ds(R0 + 4 * NC_ + m, 1)]
        GOUT = vecT[:, 1, R0 + 5 * NC_:R0 + 5 * NC_ + 1]
        RV = R0 + 5 * NC_ + 1

        w_in_p = w_in[0].rearrange("(p j) n -> p j n", j=NJ)

        s_x = [sem(f"s_x{t}") for t in range(NT)]
        s_vec = sem("s_vec")
        s_w = [sem(f"s_w{s}") for s in range(2)]
        a_norm = Steps(sem("act_norm"), ["sq0"] + [n for t in range(1, NT) for n in (f"sq{t}", f"hi{t - 1}")] + [f"hi{NT - 1}", "vecs", "w_hi"])
        g_norm = Steps(sem("pool_norm"), ["idz", "id"] + [f"{n}{t}" for t in range(NT) for n in ("ms", "rs")])
        v_norm = Steps(sem("dve_norm"), ["half"] + [f"{n}{t}" for t in range(NT) for n in ("xn", "tmp", "lo")] + ["w_lo"])
        p_norm = Steps(sem("pe_norm"), ["vecs"] + [f"T{t}" for t in range(NT)])

        with ExitStack() as c1:
            xs = qkvT[:, 0:NT, :]
            junk = zT[:, 0, :]
            xn = [zT[:, 1 + s, :] for s in range(2)]
            tmp = [convT[:, s, :].rearrange("p (j t) -> p j t", j=NJ) for s in range(2)]
            ss = sb("ss", [P, NT], ctx=c1)
            rs = sb("rs", [P, NT], ctx=c1)
            mh = sb("mh", [P, NT], ctx=c1)
            vrow = sb("vrow", [P, 2, P], ctx=c1)
            ps_v = psum("ps_v", [P, 512], ctx=c1)
            ps_x = [psum(f"ps_x{s}", [P, NJ, P], ctx=c1) for s in range(2)]
            blk = c1.enter_context(nc.Block())

            @blk.sync
            def _(sp):
                for t in range(NT):
                    sp.dma_start(xs[:, t, :], x[0, t * P:(t + 1) * P, :]).then_inc(s_x[t], 16)
                    if t == 1:
                        sp.dma_start(gmix[:], g_mix[0].rearrange("(p j) -> p j", j=NJ)).then_inc(s_loaded, 16)
                        sp.dma_start(wraw[0][:], w_in_p[:, :, GOFF:GOFF + P]).then_inc(s_w[0], 16)
                sp.dma_start(wraw[1][:], w_in_p[:, :, GOFF + CF:GOFF + CF + P]).then_inc(s_w[1], 16)

            @blk.scalar
            def _(act):
                act.dma_start(vrow[0:KC * NC_, 0, :], w_conv_dw[0].rearrange("k (m c) -> (k m) c", c=P)).then_inc(s_vec, 16)
                act.dma_start(vrow[0:R0, 1, :], w_conv_qkv[0].rearrange("k (m c) -> (k m) c", c=P)).then_inc(s_vec, 16)
                r = R0
                for v in (b_glu, b_conv_dw, ln_conv_g, ln_conv_b, g_gdn_out):
                    n = v.shape[1] // P
                    act.dma_start(vrow[r:r + n, 1, :], v[0].rearrange("(m c) -> m c", c=P)).then_inc(s_vec, 16)
                    r += n
                assert r == RV
                for t in range(NT + 1):
                    if t < NT:
                        act.wait_ge(s_x[t], 16)
                        if t:
                            act.wait_ge(*a_norm.sem_at(f"sq{t - 1}"))
                        nc.scalar.activation(junk, xs[:, t, :], ACT.Square, accum_out=ss[:, t:t + 1]).then_inc(*a_norm(f"sq{t}"))
                    if t:
                        act.wait_ge(*v_norm.sem_at(f"tmp{t - 1}"))
                        nc.scalar.activation(n1[0][:, :, (t - 1) * P:t * P], tmp[(t - 1) % 2], ACT.Copy).then_inc(*a_norm(f"hi{t - 1}"))
                act.wait_ge(*p_norm.sem_at("vecs"))
                nc.scalar.activation(vecT[:, 0, 0:KC * NC_], ps_v[:, 0:KC * NC_], ACT.Copy)
                nc.scalar.activation(vecT[:, 1, 0:RV], ps_v[:, P:P + RV], ACT.Copy).then_inc(*a_norm("vecs"))
                act.wait_ge(s_w[0], 16)
                nc.scalar.activation(wh[0][:], wraw[0][:], ACT.Copy).then_inc(*a_norm("w_hi"))

            @blk.gpsimd
            def _(pool):
                nc.gpsimd.memset(ident[:], 0.0).then_inc(*g_norm("idz"))
                pool.wait_ge(*g_norm.sem_at("idz"))
                nc.gpsimd.affine_select(out=ident[:], in_=ident[:], compare_op=ALU.not_equal, fill=1.0, base=0,
                                        pattern=[[-1, P]], channel_multiplier=1).then_inc(*g_norm("id"))
                pool.wait_ge(*v_norm.sem_at("half"))
                for t in range(NT):
                    pool.wait_ge(*a_norm.sem_at(f"sq{t}"))
                    nc.gpsimd.tensor_scalar(ss[:, t:t + 1], ss[:, t:t + 1], 1.0 / D, EPS, ALU.mult, ALU.add).then_inc(*g_norm(f"ms{t}"))
                    pool.wait_ge(*g_norm.sem_at(f"ms{t}"))
                    nc.gpsimd.tensor_tensor(rs[:, t:t + 1], ss[:, t:t + 1], mh[:, 0:1], ALU.pow).then_inc(*g_norm(f"rs{t}"))

            @blk.vector
            def _(dve):
                nc.vector.memset(mh[:], -0.5).then_inc(*v_norm("half"))
                for t in range(NT + 1):
                    if t < NT:
                        dve.wait_ge(*g_norm.sem_at(f"rs{t}"))
                        if t >= 2:
                            dve.wait_ge(*p_norm.sem_at(f"T{t - 2}"))
                        nc.vector.tensor_scalar(xn[t % 2], xs[:, t, :], rs[:, t:t + 1], None, ALU.mult).then_inc(*v_norm(f"xn{t}"))
                        dve.wait_ge(*p_norm.sem_at(f"T{t}"))
                        if t == 0:
                            dve.wait_ge(s_loaded, 16)
                        nc.vector.tensor_tensor(tmp[t % 2], ps_x[t % 2][:], gmix[:].unsqueeze(2).to_broadcast([P, NJ, P]),
                                                ALU.mult).then_inc(*v_norm(f"tmp{t}"))
                        dve.wait_ge(*a_norm.sem_at(f"hi{t}"))
                        nc.vector.tensor_tensor(n1[1][:, :, t * P:(t + 1) * P], tmp[t % 2],
                                                n1[0][:, :, t * P:(t + 1) * P].bitcast(F32), ALU.subtract).then_inc(*v_norm(f"lo{t}"))
                dve.wait_ge(*a_norm.sem_at("w_hi"))
                nc.vector.tensor_tensor(wl[0][:], wraw[0][:], wh[0][:].bitcast(F32), ALU.subtract).then_inc(*v_norm("w_lo"))

            @blk.tensor
            def _(pe):
                pe.wait_ge(*g_norm.sem_at("id"))
                pe.wait_ge(s_vec, 7 * 16)
                nc.tensor.transpose(ps_v[:, 0:KC * NC_], vrow[0:KC * NC_, 0, :], ident[0:KC * NC_, 0:KC * NC_])
                nc.tensor.transpose(ps_v[:, P:P + RV], vrow[0:RV, 1, :], ident[0:RV, 0:RV]).then_inc(*p_norm("vecs"))
                for t in range(NT):
                    pe.wait_ge(*v_norm.sem_at(f"xn{t}"))
                    if t >= 2:
                        pe.wait_ge(*v_norm.sem_at(f"tmp{t - 2}"))
                    for j in range(NJ):
                        last = nc.tensor.transpose(ps_x[t % 2][:, j, :], xn[t % 2][:, j:D:NJ], ident[:])
                    last.then_inc(*p_norm(f"T{t}"))

        NB = 6
        NI2 = NC_
        col = [lambda i: GOFF + i * P, lambda i: GOFF + CF + i * P,
               lambda i: 3 * i * P, lambda i: (3 * i + 1) * P, lambda i: (3 * i + 2) * P,
               lambda i: ZOFF + i * P]
        GROUP = 11
        a_proj = Steps(sem("act_proj"), ["hi1", "hi2", "hi3", "gate0", "gate1", "hi4", "q0", "q1",
                                         "hi5", "k0", "k1", "hi6", "v0", "v1", "z0", "z1"], credit=True)
        v_names = ["lo1", "lo2", "lo3", "u0", "u1"]
        tap_names = [f"tap{k}" for k in range(KC)]
        cuts = [0, 7, 14, 21, KC]
        for n in range(4):
            if n:
                v_names.append(f"lo{n + 3}")
            v_names += tap_names[cuts[n]:cuts[n + 1]]
        v_names += ["csum"] + [f"{c}tap{k}" for k in range(KQ) for c in "qkv"]
        v_proj = Steps(sem("dve_proj"), v_names, credit=True)
        p_proj = Steps(sem("pe_proj"), [f"b{n}" for n in range(NB)], credit=True)
        s_pad = sem("s_pad")

        with ExitStack() as c2:
            upad = sb("upad", [P, KC - 1 + T], ctx=c2)
            gate = sb("gate", [P, T], ctx=c2)
            odd = sb("odd", [P, T], ctx=c2)
            cin = [sb(f"cin{c}", [P, KQ - 1 + T], ctx=c2) for c in "qkv"]
            ps_b = [psum(f"ps_b{s}", [P, 2, 512], ctx=c2) for s in range(3)]
            ps_ba = psum("ps_ba", [P, NT, 2 * H], ctx=c2)
            s_ba = sem("s_ba")
            blk = c2.enter_context(nc.Block())

            @blk.sync
            def _(sp):
                def load(slot, freed, i, column):
                    sp.wait_ge(*v_proj.sem_at(freed, i))
                    sp.dma_start(wraw[slot][:], w_in_p[:, :, ds(column, P)]).then_inc(s_w[slot], 16)

                with sp.Fori(0, NI2 - 1) as i:
                    for n in range(NB):
                        if n + 2 < NB:
                            load(n % 2, f"lo{n}" if n else "lo6", i if n else i - 1, col[n + 2](i))
                        else:
                            load(n % 2, f"lo{n}", i, col[n + 2 - NB](i + 1))
                for n in range(NB - 2):
                    load(n % 2, f"lo{n}" if n else "lo6", NI2 - 1 if n else NI2 - 2, col[n + 2](NI2 - 1))
                load(0, f"lo{NB - 2}", NI2 - 1, BAOFF)

            @blk.scalar
            def _(act):
                a_proj.give_credit(act)
                with act.Fori(0, NI2) as i:
                    def high(n):
                        act.wait_ge(s_w[n % 2], 16 + 16 * (3 * i + n // 2))
                        act.wait_ge(*(p_proj.sem_at("b5", i - 1) if n == 1 else p_proj.sem_at(f"b{n - 2}", i)))
                        nc.scalar.activation(wh[n % 2][:], wraw[n % 2][:], ACT.Copy).then_inc(*a_proj(f"hi{n}"))

                    def drain(names, block, c):
                        act.wait_ge(*p_proj.sem_at(f"b{block}", i))
                        act.wait_ge(*v_proj.sem_at(f"{c}tap{KQ - 1}", i - 1))
                        act.wait_ge(s_pad, 1)
                        for h in range(2):
                            nc.scalar.activation(cin["qkv".index(c)][:, KQ - 1 + 512 * h:KQ - 1 + 512 * (h + 1)],
                                                 ps_b[block % 3][:, h, :], ACT.Copy).then_inc(*a_proj(names[h]))
                    high(1)
                    high(2)
                    high(3)
                    act.wait_ge(*p_proj.sem_at("b1", i))
                    act.wait_ge(*v_proj.sem_at("u1", i - 1))
                    for h in range(2):
                        nc.scalar.activation(gate[:, 512 * h:512 * (h + 1)], ps_b[1][:, h, :], ACT.Sigmoid,
                                             bias=BGLU(NC_ + i)).then_inc(*a_proj(f"gate{h}"))
                    high(4)
                    drain(("q0", "q1"), 2, "q")
                    high(5)
                    drain(("k0", "k1"), 3, "k")
                    high(6)
                    drain(("v0", "v1"), 4, "v")
                    act.wait_ge(*p_proj.sem_at("b5", i))
                    for h in range(2):
                        nc.scalar.activation(zT[:, ds(i, 1), 512 * h:512 * (h + 1)], ps_b[2][:, h:h + 1, :],
                                             ACT.Copy).then_inc(*a_proj(f"z{h}"))
                act.wait_ge(s_ba, 1)
                nc.scalar.activation(ba[:], ps_ba[:], ACT.Copy)

            @blk.vector
            def _(dve):
                v_proj.give_credit(dve)
                nc.vector.memset(upad[:, 0:KC - 1], 0.0)
                for c in range(3):
                    last = nc.vector.memset(cin[c][:, 0:KQ - 1], 0.0)
                last.then_inc(s_pad, 1)
                dve.wait_ge(s_pad, 1)
                with dve.Fori(0, NI2) as i:
                    def low(n):
                        dve.wait_ge(*a_proj.sem_at(f"hi{n}", i))
                        nc.vector.tensor_tensor(wl[n % 2][:], wraw[n % 2][:], wh[n % 2][:].bitcast(F32),
                                                ALU.subtract).then_inc(*v_proj(f"lo{n}"))

                    def tap(k):
                        dst = convT[:, ds(i, 1), :].squeeze(1) if k % 2 == 0 else odd[:]
                        src = upad[:, k:k + T]
                        if k >= 2:
                            dve.wait_ge(*v_proj.sem_at(f"tap{k - 2}", i))
                            ins = nc.vector.scalar_tensor_tensor(dst, src, DW(k, i), dst, ALU.mult, ALU.add)
                        elif k == 0:
                            ins = nc.vector.tensor_scalar(dst, src, DW(k, i), BDW(i), ALU.mult, ALU.add)
                        else:
                            ins = nc.vector.tensor_scalar(dst, src, DW(k, i), None, ALU.mult)
                        ins.then_inc(*v_proj(f"tap{k}"))

                    low(1)
                    low(2)
                    low(3)
                    for h in range(2):
                        dve.wait_ge(*a_proj.sem_at(f"gate{h}", i))
                        nc.vector.scalar_tensor_tensor(upad[:, KC - 1 + 512 * h:KC - 1 + 512 * (h + 1)], ps_b[0][:, h, :],
                                                       BGLU(i), gate[:, 512 * h:512 * (h + 1)], ALU.add,
                                                       ALU.mult).then_inc(*v_proj(f"u{h}"))
                    dve.wait_ge(*v_proj.sem_at("u1", i))
                    for n in range(4):
                        if n:
                            low(n + 3)
                        for k in range(cuts[n], cuts[n + 1]):
                            tap(k)
                    c = convT[:, ds(i, 1), :].squeeze(1)
                    dve.wait_ge(*v_proj.sem_at(f"tap{KC - 1}", i))
                    nc.vector.tensor_tensor(c, c, odd[:], ALU.add).then_inc(*v_proj("csum"))
                    for k in range(KQ):
                        for c in range(3):
                            dst = qkvT[:, ds(3 * i + c, 1), :].squeeze(1)
                            src = cin[c][:, k:k + T]
                            if k == 0:
                                dve.wait_ge(*a_proj.sem_at(f"{'qkv'[c]}1", i))
                                ins = nc.vector.tensor_scalar(dst, src, CQ(0, 3 * i + c), None, ALU.mult)
                            else:
                                dve.wait_ge(*v_proj.sem_at(f"{'qkv'[c]}tap{k - 1}", i))
                                ins = nc.vector.scalar_tensor_tensor(dst, src, CQ(k, 3 * i + c), dst, ALU.mult, ALU.add)
                            ins.then_inc(*v_proj(f"{'qkv'[c]}tap{k}"))

            @blk.tensor
            def _(pe):
                p_proj.give_credit(pe)
                drained = [(v_proj, "u1"), (a_proj, "gate1"), (a_proj, "q1"), (a_proj, "k1"), (a_proj, "v1"), (a_proj, "z1")]
                with pe.Fori(0, NI2) as i:
                    for n in range(NB):
                        if n == 0:
                            pe.wait_ge(*a_proj.sem_at("hi6", i - 1))
                            pe.wait_ge(*v_proj.sem_at("lo6", i - 1))
                        else:
                            pe.wait_ge(*v_proj.sem_at(f"lo{n}", i))
                        who, step = drained[(n + 3) % NB]
                        pe.wait_ge(*who.sem_at(step, i - 1 if n < 3 else i))
                        for h in range(2):
                            for j in range(NJ):
                                last = mm3(ps_b[n % 3][:, h, :], [wh[n % 2][:, j, :], wl[n % 2][:, j, :]],
                                           [n1[0][:, j, 512 * h:512 * (h + 1)], n1[1][:, j, 512 * h:512 * (h + 1)]],
                                           j == 0, j == NJ - 1)
                        last.then_inc(*p_proj(f"b{n}"))
                pe.wait_ge(*v_proj.sem_at("lo6", NI2 - 1))
                for t in range(NT):
                    for j in range(NJ):
                        tok = slice(t * P, (t + 1) * P)
                        last = mm3(ps_ba[:, t, :], [n1[0][:, j, tok], n1[1][:, j, tok]],
                                   [wh[0][:, j, 0:2 * H], wl[0][:, j, 0:2 * H]], j == 0, j == NJ - 1)
                last.then_inc(s_ba, 1)
        n1ctx.close()

        gdn = ExitStack()
        TH = NT * H
        dti = sb("dti", [P, TH, CH], ctx=gdn)
        dts = sb("dts", [P, TH, CH], ctx=gdn)
        egt = sb("egt", [P, TH, P], ctx=gdn)
        beta = sb("beta", [P, NT, H], ctx=gdn)
        bege = sb("bege", [P, NT, H], ctx=gdn)
        edec = sb("edec", [P, NT, H], ctx=gdn)
        gtb = sb("gtb", [P, 2, TH], ctx=gdn)
        lev = sb("lev", [P, 6, CH], ctx=gdn)
        eye2 = sb("eye2", [P, CH], ctx=gdn)
        mhalf = sb("mhalf", [P, 2 * H], ctx=gdn)
        epst = sb("epst", [P, 2 * H], ctx=gdn)
        qscale = sb("qscale", [P, H], ctx=gdn)
        HB = [slice(0, CH), slice(CH, P)]

        s_dec = sem("s_dec")
        HF = [slice(0, 512), slice(512, 1024)]
        p_pre = Steps(sem("pe_pre"), ["sum0", "sum1", "D0", "B0", "E0", "gt0", "small", "D1", "B1", "E1", "var0", "var1",
                                      "D2", "B2", "E2", "D3", "B3", "E3"])
        v_pre = Steps(sem("dve_pre"), ["dev0", "dev1", "y", "ay", "be1", "beta", "ry", "sp", "g", "GT", "BI"]
                      + ["dm0", "bs0", "dm1", "bs1", "var0", "var1", "bege", "gc", "dgc"]
                      + ["dm2", "bs2", "dm3", "bs3", "rc0", "rc1", "nrm0", "nrm1"])
        a_pre = Steps(sem("act_pre"), ["ea", "eb", "ey", "ln", "sq0", "sq1", "di0", "eg0", "gce", "gtb", "di1", "eg1",
                                       "edec", "di2", "eg2", "di3", "eg3", "sd0", "sd1", "silu"])
        s_masks = sem("s_masks")
        MASKS = 9 + 2 * 4

        with ExitStack() as c3:
            ones = sb("ones", [P, P], ctx=c3)
            tri = sb("tri", [P, CH], ctx=c3)
            ntri = sb("ntri", [P, CH], ctx=c3)
            negm = sb("negm", [P, CH], ctx=c3)
            alog = sb("alog", [P, H], ctx=c3)
            dtb = sb("dtb", [P, H], ctx=c3)
            ea = sb("ea", [P, H], ctx=c3)
            sm = {n: sb("sm_" + n, [P, NT, H], ctx=c3) for n in ("y", "ay", "ey", "ln", "eb", "b1", "g", "gce", "dgc")}
            GT = sb("GT", [P, TH, CH], ctx=c3)
            BI = sb("BI", [P, TH, CH], ctx=c3)
            dm = [sb(f"dm{s}", [P, 8, CH], ctx=c3) for s in range(2)]
            sq = sb("sq", [P, NC_, T], ctx=c3)
            vr = sb("vr", [P, T], ctx=c3)
            mh2 = sb("mh2", [P, 1], ctx=c3)
            ps_s = [psum(f"ps_s{h}", [P, 512], ctx=c3) for h in range(2)]
            ps_D = [psum(f"ps_D{h}", [P, 8, CH], ctx=c3) for h in range(2)]
            ps_B = psum("ps_B", [P, 8, CH], ctx=c3)
            ps_E = [psum(f"ps_E{h}", [P, 8, P // 2], ctx=c3) for h in range(2)]
            ps_m = psum("ps_m", [P, 4, TH], ctx=c3)
            blk = c3.enter_context(nc.Block())

            @blk.sync
            def _(sp):
                sp.dma_start(alog[:], a_log.partition_broadcast(P)).then_inc(s_dec, 16)
                sp.dma_start(dtb[:], dt_bias.partition_broadcast(P)).then_inc(s_dec, 16)

            @blk.gpsimd
            def _(pool):
                done = 0

                def alone(ins):
                    nonlocal done
                    done += 1
                    ins.then_inc(s_masks, 1)
                    pool.wait_ge(s_masks, done)

                for m, v in ((ones, 1.0), (mh2, -0.5), (mhalf, -0.5), (epst, EPS), (qscale, float(DK) ** -0.5), (eye2, 0.0), (tri, 1.0), (ntri, -1.0), (negm, 0.0)):
                    alone(nc.gpsimd.memset(m[:], v))
                for b in HB:
                    for m, fill in ((tri, 0.0), (ntri, 0.0), (negm, NEG)):
                        alone(nc.gpsimd.affine_select(out=m[b, :], in_=m[b, :], compare_op=ALU.is_ge, fill=fill, base=0,
                                                      pattern=[[1, CH]], channel_multiplier=-1))
                    alone(nc.gpsimd.affine_select(out=eye2[b, :], in_=eye2[b, :], compare_op=ALU.not_equal, fill=1.0, base=0,
                                                  pattern=[[-1, CH]], channel_multiplier=1))
                masks_ready = done
                assert masks_ready == MASKS
                alone(nc.gpsimd.memset(lev[:], 0.0))
                for l in range(6):
                    w = 1 << l
                    nb = CH // (2 * w)
                    for b in HB:
                        m = lev[b, l, :].rearrange("p (n two w) -> p n two w", two=2, w=w)[:, :, 1, :]
                        alone(nc.gpsimd.memset(m, 1.0))
                        alone(nc.gpsimd.affine_select(out=m, in_=m, compare_op=ALU.is_ge, fill=0.0, base=0,
                                                      pattern=[[-2 * w, nb], [0, w]], channel_multiplier=1))
                        alone(nc.gpsimd.affine_select(out=m, in_=m, compare_op=ALU.is_ge, fill=0.0, base=w - 1,
                                                      pattern=[[2 * w, nb], [0, w]], channel_multiplier=-1))

            @blk.tensor
            def _(pe):
                pe.wait_ge(s_masks, 1)
                for h in range(2):
                    for m in range(NC_):
                        last = nc.tensor.matmul(ps_s[h][:], ones[:], convT[:, m, HF[h]], start=m == 0, stop=m == NC_ - 1)
                    last.then_inc(*p_pre(f"sum{h}"))
                pe.wait_ge(s_masks, MASKS)

                def decays(q):
                    hq = slice(8 * q, 8 * q + 8)
                    pe.wait_ge(*v_pre.sem_at("BI"))
                    if q >= 2:
                        pe.wait_ge(*v_pre.sem_at(f"dm{q - 2}"))
                    for b in HB:
                        nc.tensor.matmul(ps_D[q % 2][b, :, :], ones[b, 0:CH], GT[b, hq, :], start=True, stop=False)
                        last = nc.tensor.matmul(ps_D[q % 2][b, :, :], ntri[b, :],
                                                g8(b, hq), start=False, stop=True)
                    last.then_inc(*p_pre(f"D{q}"))
                    if q >= 1:
                        pe.wait_ge(*v_pre.sem_at(f"bs{q - 1}"))
                    for b in HB:
                        last = nc.tensor.matmul(ps_B[b, :, :], ones[b, 0:CH], BI[b, hq, :], start=True, stop=True)
                    last.then_inc(*p_pre(f"B{q}"))
                    if q >= 1:
                        pe.wait_ge(*a_pre.sem_at(f"eg{q - 1}"))
                    for n, b in enumerate(HB):
                        last = nc.tensor.matmul(ps_E[n][:], ones[b, :], GT[b, hq, :], start=True, stop=True)
                    last.then_inc(*p_pre(f"E{q}"))

                def g8(b, hq):
                    return sm["g"][:].rearrange("p t h -> p (t h)")[b, hq].unsqueeze(2).to_broadcast([CH, 8, CH])

                decays(0)
                gf = sm["g"][:].rearrange("p t h -> p (t h)")
                for n, b in enumerate(HB):
                    nc.tensor.matmul(ps_m[b, 0, :], tri[b, :], gf[b, :], start=True, stop=True)
                    nc.tensor.matmul(ps_m[b, 1, :], ones[b, 0:CH], gf[b, :], start=True, stop=True)
                nc.tensor.matmul(ps_m[:, 2, :], ones[HB[0], :], gf[HB[0], :], start=True, stop=True).then_inc(*p_pre("gt0"))
                pe.wait_ge(*p_pre.sem_at("gt0"))
                nc.tensor.matmul(ps_m[:, 3, :], ones[HB[1], :], gf[HB[1], :], start=True, stop=True).then_inc(*p_pre("small"))
                decays(1)
                for h in range(2):
                    pe.wait_ge(*a_pre.sem_at(f"sq{h}"))
                    for m in range(NC_):
                        last = nc.tensor.matmul(ps_s[h][:], ones[:], sq[:, m, HF[h]], start=m == 0, stop=m == NC_ - 1)
                    last.then_inc(*p_pre(f"var{h}"))
                decays(2)
                decays(3)

            @blk.scalar
            def _(act):
                act.wait_ge(s_dec, 32)
                nc.scalar.activation(ea[:], alog[:], ACT.Exp).then_inc(*a_pre("ea"))
                nc.scalar.activation(sm["eb"][:], ba[:, :, 0:H], ACT.Exp, scale=-1.0).then_inc(*a_pre("eb"))
                act.wait_ge(*v_pre.sem_at("ay"))
                nc.scalar.activation(sm["ey"][:], sm["ay"][:], ACT.Exp, scale=-1.0).then_inc(*a_pre("ey"))
                act.wait_ge(*a_pre.sem_at("ey"))
                nc.scalar.activation(sm["ln"][:], sm["ey"][:], ACT.Ln, bias=1.0).then_inc(*a_pre("ln"))
                for h in range(2):
                    act.wait_ge(*v_pre.sem_at(f"dev{h}"))
                    nc.scalar.activation(sq[:, :, HF[h]], convT[:, :, HF[h]], ACT.Square).then_inc(*a_pre(f"sq{h}"))

                def decays(q):
                    act.wait_ge(*v_pre.sem_at(f"dm{q}"))
                    nc.scalar.activation(dti[:, 8 * q:8 * q + 8, :], dm[q % 2][:], ACT.Exp).then_inc(*a_pre(f"di{q}"))
                    act.wait_ge(*p_pre.sem_at(f"E{q}"))
                    for b in range(2):
                        last = nc.scalar.activation(egt[:, 8 * q:8 * q + 8, HB[b]], ps_E[b][:], ACT.Exp)
                    last.then_inc(*a_pre(f"eg{q}"))

                decays(0)
                act.wait_ge(*p_pre.sem_at("small"))
                nc.scalar.activation(sm["gce"][:].rearrange("p t h -> p (t h)"), ps_m[:, 0, :], ACT.Exp).then_inc(*a_pre("gce"))
                nc.scalar.activation(gtb[:], ps_m[:, 2:4, :], ACT.Exp).then_inc(*a_pre("gtb"))
                decays(1)
                act.wait_ge(*v_pre.sem_at("dgc"))
                nc.scalar.activation(edec[:], sm["dgc"][:], ACT.Exp).then_inc(*a_pre("edec"))
                decays(2)
                decays(3)
                for h in range(2):
                    act.wait_ge(*v_pre.sem_at(f"var{h}"))
                    nc.scalar.activation(vr[:, HF[h]], vr[:, HF[h]], ACT.Sqrt).then_inc(*a_pre(f"sd{h}"))
                for m in range(NC_):
                    act.wait_ge(*v_pre.sem_at("nrm1"))
                    last = nc.scalar.activation(convT[:, m, :], convT[:, m, :], ACT.Silu, scale=LNG(m), bias=LNB(m))
                last.then_inc(*a_pre("silu"))

            @blk.vector
            def _(dve):
                def flat(t):
                    return t[:].rearrange("p t h -> p (t h)")

                for h in range(2):
                    dve.wait_ge(*p_pre.sem_at(f"sum{h}"))
                    for m in range(NC_):
                        last = nc.vector.scalar_tensor_tensor(convT[:, m, HF[h]], ps_s[h][:], -1.0 / CF, convT[:, m, HF[h]],
                                                              ALU.mult, ALU.add)
                    last.then_inc(*v_pre(f"dev{h}"))
                dve.wait_ge(s_dec, 32)
                hb = [P, NT, H]
                nc.vector.tensor_tensor(sm["y"][:], ba[:, :, H:2 * H], dtb[:].unsqueeze(1).to_broadcast(hb), ALU.add).then_inc(*v_pre("y"))
                dve.wait_ge(*v_pre.sem_at("y"))
                nc.vector.scalar_tensor_tensor(sm["ay"][:], sm["y"][:], -1.0, sm["y"][:], ALU.mult, ALU.max).then_inc(*v_pre("ay"))
                dve.wait_ge(*a_pre.sem_at("eb"))
                nc.vector.tensor_scalar(sm["b1"][:], sm["eb"][:], 1.0, None, ALU.add).then_inc(*v_pre("be1"))
                dve.wait_ge(*v_pre.sem_at("be1"))
                nc.vector.reciprocal(beta[:], sm["b1"][:]).then_inc(*v_pre("beta"))
                nc.vector.tensor_scalar(sm["y"][:], sm["y"][:], 0.0, None, ALU.max).then_inc(*v_pre("ry"))
                dve.wait_ge(*a_pre.sem_at("ln"))
                dve.wait_ge(*v_pre.sem_at("ry"))
                nc.vector.tensor_tensor(sm["y"][:], sm["y"][:], sm["ln"][:], ALU.add).then_inc(*v_pre("sp"))
                dve.wait_ge(*v_pre.sem_at("sp"))
                nc.vector.scalar_tensor_tensor(sm["g"][:], sm["y"][:], -1.0, ea[:].unsqueeze(1).to_broadcast(hb),
                                               ALU.mult, ALU.mult).then_inc(*v_pre("g"))
                dve.wait_ge(*v_pre.sem_at("g"))
                dve.wait_ge(s_masks, MASKS)
                wide = [P, TH, CH]
                nc.vector.tensor_tensor(GT[:], flat(sm["g"]).unsqueeze(2).to_broadcast(wide),
                                        tri[:].unsqueeze(1).to_broadcast(wide), ALU.mult).then_inc(*v_pre("GT"))
                nc.vector.tensor_tensor(BI[:], flat(beta).unsqueeze(2).to_broadcast(wide),
                                        eye2[:].unsqueeze(1).to_broadcast(wide), ALU.mult).then_inc(*v_pre("BI"))

                def decays(q):
                    dve.wait_ge(*p_pre.sem_at(f"D{q}"))
                    if q >= 2:
                        dve.wait_ge(*a_pre.sem_at(f"di{q - 2}"))
                    nc.vector.tensor_tensor(dm[q % 2][:], ps_D[q % 2][:], negm[:].unsqueeze(1).to_broadcast([P, 8, CH]),
                                            ALU.add).then_inc(*v_pre(f"dm{q}"))
                    dve.wait_ge(*p_pre.sem_at(f"B{q}"))
                    dve.wait_ge(*a_pre.sem_at(f"di{q}"))
                    nc.vector.tensor_tensor(dts[:, 8 * q:8 * q + 8, :], dti[:, 8 * q:8 * q + 8, :], ps_B[:],
                                            ALU.mult).then_inc(*v_pre(f"bs{q}"))

                decays(0)
                decays(1)
                for h in range(2):
                    dve.wait_ge(*p_pre.sem_at(f"var{h}"))
                    nc.vector.tensor_scalar(vr[:, HF[h]], ps_s[h][:], 1.0 / CF, EPS, ALU.mult, ALU.add).then_inc(*v_pre(f"var{h}"))
                dve.wait_ge(*a_pre.sem_at("gtb"))
                nc.vector.tensor_tensor(bege[:], beta[:], sm["gce"][:], ALU.mult).then_inc(*v_pre("bege"))
                nc.vector.tensor_copy(flat(sm["b1"]), ps_m[:, 0, :]).then_inc(*v_pre("gc"))
                dve.wait_ge(*v_pre.sem_at("gc"))
                nc.vector.tensor_tensor(flat(sm["dgc"]), ps_m[:, 1, :], flat(sm["b1"]), ALU.subtract).then_inc(*v_pre("dgc"))
                decays(2)
                decays(3)
                for h in range(2):
                    dve.wait_ge(*a_pre.sem_at(f"sd{h}"))
                    nc.vector.reciprocal(vr[:, HF[h]], vr[:, HF[h]]).then_inc(*v_pre(f"rc{h}"))
                for h in range(2):
                    dve.wait_ge(*v_pre.sem_at(f"rc{h}"))
                    hw = [P, NC_, 512]
                    nc.vector.tensor_tensor(convT[:, :, HF[h]], convT[:, :, HF[h]], vr[:, HF[h]].unsqueeze(1).to_broadcast(hw),
                                            ALU.mult).then_inc(*v_pre(f"nrm{h}"))

        G2 = range(2)
        LV = range(1, 6)
        F4 = [P, H, P]
        H4 = [P, H, CH]

        def both(names):
            return [f"{n}{g}" for n in names for g in G2]

        a_names = both(["silq", "silk", "silv", "sqq", "sqk", "knT", "qnT"])
        for l in LV:
            a_names += both([f"U{l}"])
        a_names += both(["u", "wT0", "wT1", "zs"]) + ["sqo0", "sqo1"]
        a_gdn = Steps(sem("act_gdn"), a_names, credit=True)
        v_names = both(["ss", "qn", "kn", "vb", "LT", "QKT", "Y0", "X0"])
        for l in LV:
            v_names += both([f"Y{l}"] + ([f"X{l}"] if l < 5 else []))
        for g in G2:
            for b in G2:
                v_names += [f"vn{b}{g}"] + [f"S{h}{b}{g}" for h in range(H)]
            v_names += [f"so{g}", f"on{g}", f"y{g}"]
        v_gdn = Steps(sem("dve_gdn"), v_names, credit=True)
        g_names = both(["ms", "rr", "qs"]) + both(["kw", "kd", "qd"]) + both([f"m{l}" for l in range(6)])
        for g in G2:
            g_names += [f"mo{g}", f"ro{g}"]
        g_gdn = Steps(sem("pool_gdn"), g_names, credit=True)
        p_names = both(["tq", "tk", "tv", "tkn", "tqn", "A", "QK", "X0"])
        for l in LV:
            p_names += both([f"U{l}"] + ([f"X{l}"] if l < 5 else []) + [f"Y{l}"])
        p_names += both(["u", "wT0", "wT1"])
        for g in G2:
            for b in G2:
                p_names += [f"W{b}{g}", f"dS{b}{g}", f"o{b}{g}"]
            p_names += [f"ty{g}"]
        p_gdn = Steps(sem("pe_gdn"), p_names, credit=True)

        with ExitStack() as c4:
            def two(name, shape):
                return [sb(f"{name}_{g}", shape, ctx=c4) for g in G2]

            qkvs = two("qkvs", [P, 3 * H, P])
            sqs = [t[:, 0:2 * H] for t in qkvs]
            ssq = two("ssq", [P, 2 * H])
            rr = two("rr", [P, 2 * H])
            so = two("so", [P, H])
            ro = two("ro", [P, H])
            qn, kn, kw, kd, vb = (two(n, F4) for n in ("qn", "kn", "kw", "kd", "vb"))
            knT, qnT, qdT = (two(n, F4) for n in ("knT", "qnT", "qdT"))
            LT, QKT, X, Y, U = (two(n, H4) for n in ("LT", "QKT", "X", "Y", "U"))
            ml = two("ml", [P, 6, H, CH])
            us, vn = two("us", F4), two("vn", F4)
            wT = two("wT", [P, 2, H, CH])
            zs = two("zs", F4)
            S = two("S", F4)
            bank = [[psum(f"ps_g{g}{k}", [P, H, P], ctx=c4) for k in range(4)] for g in G2]
            half = [[b[:].rearrange("p h c -> p (h c)")[:, 0:H * CH].rearrange("p (h c) -> p h c", h=H) for b in bk] for bk in bank]
            s_zero = sem("s_zero")
            blk = c4.enter_context(nc.Block())

            def tile_rows(t, i, g):
                return t[:, ds((2 * i + g) * H, H), :]

            @blk.scalar
            def _(act):
                a_gdn.give_credit(act)
                with act.Fori(0, NT // 2) as i:
                    for n, c in enumerate("qkv"):
                        for g in G2:
                            if n == 0:
                                act.wait_ge(*v_gdn.sem_at(f"y{g}", i - 1))
                            nc.scalar.activation(qkvs[g][:, H * n:H * (n + 1), :], qkvT[:, H * n:H * (n + 1), ds((2 * i + g) * P, P)],
                                                 ACT.Silu).then_inc(*a_gdn(f"sil{c}{g}"))
                    for n, c in enumerate("qk"):
                        for g in G2:
                            act.wait_ge(*p_gdn.sem_at(f"t{c}{g}", i))
                            nc.scalar.activation(sqs[g][:, H * n:H * (n + 1), :], bank[g][n][:], ACT.Square).then_inc(*a_gdn(f"sq{c}{g}"))
                    for g in G2:
                        act.wait_ge(*p_gdn.sem_at(f"tkn{g}", i))
                        nc.scalar.activation(knT[g][:], bank[g][3][:], ACT.Copy).then_inc(*a_gdn(f"knT{g}"))
                    for g in G2:
                        act.wait_ge(*p_gdn.sem_at(f"tqn{g}", i))
                        nc.scalar.activation(qnT[g][:], bank[g][0][:], ACT.Copy).then_inc(*a_gdn(f"qnT{g}"))
                    for l in LV:
                        for g in G2:
                            act.wait_ge(*p_gdn.sem_at(f"U{l}{g}", i))
                            nc.scalar.activation(U[g][:], half[g][3], ACT.Copy).then_inc(*a_gdn(f"U{l}{g}"))
                    for g in G2:
                        act.wait_ge(*p_gdn.sem_at(f"u{g}", i))
                        nc.scalar.activation(us[g][:], bank[g][1][:], ACT.Copy).then_inc(*a_gdn(f"u{g}"))
                    for b in G2:
                        for g in G2:
                            act.wait_ge(*p_gdn.sem_at(f"wT{b}{g}", i))
                            nc.scalar.activation(wT[g][:, b], half[g][2 + b], ACT.Copy).then_inc(*a_gdn(f"wT{b}{g}"))
                    for g in G2:
                        nc.scalar.activation(zs[g][:], zT[:, :, ds((2 * i + g) * P, P)], ACT.Silu).then_inc(*a_gdn(f"zs{g}"))
                    for g in G2:
                        act.wait_ge(*p_gdn.sem_at(f"o1{g}", i))
                        nc.scalar.activation(sqs[g][:, 0:H, :], bank[g][0][:], ACT.Square, scale=float(DK) ** -0.5).then_inc(*a_gdn(f"sqo{g}"))

            @blk.gpsimd
            def _(pool):
                g_gdn.give_credit(pool)
                with pool.Fori(0, NT // 2) as i:
                    for g in G2:
                        pool.wait_ge(*v_gdn.sem_at(f"ss{g}", i))
                        nc.gpsimd.tensor_tensor(ssq[g][:], ssq[g][:], epst[:], ALU.add).then_inc(*g_gdn(f"ms{g}"))
                    for g in G2:
                        pool.wait_ge(*g_gdn.sem_at(f"ms{g}", i))
                        nc.gpsimd.tensor_tensor(rr[g][:], ssq[g][:], mhalf[:], ALU.pow).then_inc(*g_gdn(f"rr{g}"))
                    for g in G2:
                        pool.wait_ge(*g_gdn.sem_at(f"rr{g}", i))
                        nc.gpsimd.tensor_tensor(rr[g][:, 0:H], rr[g][:, 0:H], qscale[:], ALU.mult).then_inc(*g_gdn(f"qs{g}"))
                    for g in G2:
                        pool.wait_ge(*v_gdn.sem_at(f"kn{g}", i))
                        nc.gpsimd.tensor_tensor(kw[g][:], kn[g][:], bege[:, ds(2 * i + g, 1), :].squeeze(1).unsqueeze(2).to_broadcast(F4),
                                                ALU.mult).then_inc(*g_gdn(f"kw{g}"))
                    for g in G2:
                        nc.gpsimd.tensor_tensor(kd[g][:], kn[g][:], edec[:, ds(2 * i + g, 1), :].squeeze(1).unsqueeze(2).to_broadcast(F4),
                                                ALU.mult).then_inc(*g_gdn(f"kd{g}"))
                    for g in G2:
                        pool.wait_ge(*a_gdn.sem_at(f"qnT{g}", i))
                        nc.gpsimd.tensor_tensor(qdT[g][:], qnT[g][:], tile_rows(egt, i, g), ALU.mult).then_inc(*g_gdn(f"qd{g}"))
                    for l in range(6):
                        for g in G2:
                            pool.wait_ge(*v_gdn.sem_at(f"LT{g}", i))
                            nc.gpsimd.tensor_tensor(ml[g][:, l], LT[g][:], lev[:, l:l + 1, :].to_broadcast(H4), ALU.mult).then_inc(*g_gdn(f"m{l}{g}"))
                    for g in G2:
                        pool.wait_ge(*v_gdn.sem_at(f"so{g}", i))
                        nc.gpsimd.tensor_tensor(so[g][:], so[g][:], epst[:, 0:H], ALU.add).then_inc(*g_gdn(f"mo{g}"))
                        pool.wait_ge(*g_gdn.sem_at(f"mo{g}", i))
                        nc.gpsimd.tensor_tensor(ro[g][:], so[g][:], mhalf[:, 0:H], ALU.pow).then_inc(*g_gdn(f"ro{g}"))

            @blk.vector
            def _(dve):
                def bc(a):
                    return a.unsqueeze(2).to_broadcast(F4)

                nc.vector.memset(S[0][:], 0.0).then_inc(s_zero, 1)
                v_gdn.give_credit(dve)
                with dve.Fori(0, NT // 2) as i:
                    for g in G2:
                        dve.wait_ge(*a_gdn.sem_at(f"sqk{g}", i))
                        nc.vector.tensor_reduce(ssq[g][:], sqs[g], axis=AX.X, op=ALU.add).then_inc(*v_gdn(f"ss{g}"))
                    for g in G2:
                        dve.wait_ge(*g_gdn.sem_at(f"qs{g}", i))
                        nc.vector.tensor_tensor(qn[g][:], bank[g][0][:], bc(rr[g][:, 0:H]), ALU.mult).then_inc(*v_gdn(f"qn{g}"))
                    for g in G2:
                        nc.vector.tensor_tensor(kn[g][:], bank[g][1][:], bc(rr[g][:, H:2 * H]), ALU.mult).then_inc(*v_gdn(f"kn{g}"))
                    for g in G2:
                        dve.wait_ge(*p_gdn.sem_at(f"tv{g}", i))
                        nc.vector.tensor_tensor(vb[g][:], bank[g][2][:], bc(beta[:, ds(2 * i + g, 1), :].squeeze(1)), ALU.mult).then_inc(*v_gdn(f"vb{g}"))
                    for g in G2:
                        dve.wait_ge(*p_gdn.sem_at(f"A{g}", i))
                        nc.vector.tensor_tensor(LT[g][:], half[g][1], tile_rows(dts, i, g), ALU.mult).then_inc(*v_gdn(f"LT{g}"))
                    for g in G2:
                        dve.wait_ge(*p_gdn.sem_at(f"QK{g}", i))
                        nc.vector.tensor_tensor(QKT[g][:], half[g][2], tile_rows(dti, i, g), ALU.mult).then_inc(*v_gdn(f"QKT{g}"))
                    for g in G2:
                        dve.wait_ge(*g_gdn.sem_at(f"m0{g}", i))
                        nc.vector.tensor_tensor(Y[g][:], eye2[:].unsqueeze(1).to_broadcast(H4), ml[g][:, 0], ALU.subtract).then_inc(*v_gdn(f"Y0{g}"))
                    for g in G2:
                        dve.wait_ge(*p_gdn.sem_at(f"X0{g}", i))
                        nc.vector.tensor_tensor(X[g][:], eye2[:].unsqueeze(1).to_broadcast(H4), half[g][2], ALU.subtract).then_inc(*v_gdn(f"X0{g}"))
                    for l in LV:
                        for g in G2:
                            dve.wait_ge(*p_gdn.sem_at(f"Y{l}{g}", i))
                            nc.vector.tensor_tensor(Y[g][:], Y[g][:], half[g][0], ALU.subtract).then_inc(*v_gdn(f"Y{l}{g}"))
                        if l < 5:
                            for g in G2:
                                dve.wait_ge(*p_gdn.sem_at(f"X{l}{g}", i))
                                nc.vector.tensor_tensor(X[g][:], X[g][:], half[g][2], ALU.subtract).then_inc(*v_gdn(f"X{l}{g}"))
                    for g in G2:
                        for b in G2:
                            r = HB[b]
                            dve.wait_ge(*p_gdn.sem_at(f"W{b}{g}", i))
                            nc.vector.tensor_tensor(vn[g][r], us[g][r], bank[g][3][r], ALU.subtract).then_inc(*v_gdn(f"vn{b}{g}"))
                            dve.wait_ge(*p_gdn.sem_at(f"dS{b}{g}", i))
                            for h in range(H):
                                nc.vector.scalar_tensor_tensor(S[1 - b][:, h], S[b][:, h], gtb[:, b, ds((2 * i + g) * H + h, 1)],
                                                               bank[g][2][:, h], ALU.mult, ALU.add).then_inc(*v_gdn(f"S{h}{b}{g}"))
                        dve.wait_ge(*a_gdn.sem_at(f"sqo{g}", i))
                        nc.vector.tensor_reduce(so[g][:], sqs[g][:, 0:H], axis=AX.X, op=ALU.add).then_inc(*v_gdn(f"so{g}"))
                        dve.wait_ge(*g_gdn.sem_at(f"ro{g}", i))
                        nc.vector.tensor_tensor(qn[g][:], bank[g][0][:], bc(ro[g][:]), ALU.mult).then_inc(*v_gdn(f"on{g}"))
                        dve.wait_ge(*p_gdn.sem_at(f"ty{g}", i))
                        nc.vector.scalar_tensor_tensor(zT[:, :, ds((2 * i + g) * P, P)], bank[g][1][:], GOUT, zs[g][:],
                                                       ALU.mult, ALU.mult).then_inc(*v_gdn(f"y{g}"))

            @blk.tensor
            def _(pe):
                def heads(f):
                    for h in range(H):
                        last = f(h)
                    return last

                def blocks(f):
                    for b in HB:
                        for h in range(H):
                            last = f(b, h)
                    return last

                def wait_here(sem, value):
                    pe.wait_ge(sem, value)
                    pe.sem_inc(s_turn, 1)

                def mm(out, a, b, start=True, stop=True):
                    return nc.tensor.matmul(out, a, b, start=start, stop=stop)

                p_gdn.give_credit(pe)
                pe.wait_ge(s_zero, 1)
                with pe.Fori(0, NT // 2) as i:
                    for n, c in enumerate("qkv"):
                        for g in G2:
                            pe.wait_ge(*a_gdn.sem_at(f"sil{c}{g}", i))
                            heads(lambda h: nc.tensor.transpose(bank[g][n][:, h], qkvs[g][:, H * n + h], ident[:])).then_inc(*p_gdn(f"t{c}{g}"))
                    for g in G2:
                        pe.wait_ge(*v_gdn.sem_at(f"kn{g}", i))
                        heads(lambda h: nc.tensor.transpose(bank[g][3][:, h], kn[g][:, h], ident[:])).then_inc(*p_gdn(f"tkn{g}"))
                    for g in G2:
                        heads(lambda h: nc.tensor.transpose(bank[g][0][:, h], qn[g][:, h], ident[:])).then_inc(*p_gdn(f"tqn{g}"))
                    for g in G2:
                        pe.wait_ge(*a_gdn.sem_at(f"knT{g}", i))
                        blocks(lambda b, h: mm(half[g][1][b, h], knT[g][:, h, b], knT[g][:, h, b])).then_inc(*p_gdn(f"A{g}"))
                    for g in G2:
                        pe.wait_ge(*a_gdn.sem_at(f"qnT{g}", i))
                        pe.wait_ge(*v_gdn.sem_at(f"vb{g}", i))
                        blocks(lambda b, h: mm(half[g][2][b, h], knT[g][:, h, b], qnT[g][:, h, b])).then_inc(*p_gdn(f"QK{g}"))
                    for g in G2:
                        pe.wait_ge(*g_gdn.sem_at(f"m0{g}", i))
                        wait_here(*v_gdn.sem_at(f"QKT{g}", i))
                        blocks(lambda b, h: mm(half[g][2][b, h], ml[g][b, 0, h], eye2[b])).then_inc(*p_gdn(f"X0{g}"))
                    for l in LV:
                        for g in G2:
                            pe.wait_ge(*g_gdn.sem_at(f"m{l}{g}", i))
                            wait_here(*v_gdn.sem_at(f"X{l - 1}{g}", i))
                            blocks(lambda b, h: mm(half[g][3][b, h], ml[g][b, l, h], X[g][b, h])).then_inc(*p_gdn(f"U{l}{g}"))
                        for g in G2:
                            if l < 5:
                                wait_here(*a_gdn.sem_at(f"U{l}{g}", i))
                                blocks(lambda b, h: mm(half[g][2][b, h], Y[g][b, h], U[g][b, h])).then_inc(*p_gdn(f"X{l}{g}"))
                        for g in G2:
                            wait_here(*a_gdn.sem_at(f"U{l}{g}", i))
                            blocks(lambda b, h: mm(half[g][0][b, h], U[g][b, h], Y[g][b, h])).then_inc(*p_gdn(f"Y{l}{g}"))
                    for g in G2:
                        wait_here(*v_gdn.sem_at(f"Y5{g}", i))
                        blocks(lambda b, h: mm(bank[g][1][b, h], Y[g][b, h], vb[g][b, h])).then_inc(*p_gdn(f"u{g}"))
                    for b in G2:
                        for g in G2:
                            pe.wait_ge(*g_gdn.sem_at(f"kw{g}", i))
                            heads(lambda h: mm(half[g][2 + b][:, h], kw[g][HB[b], h], Y[g][HB[b], h])).then_inc(*p_gdn(f"wT{b}{g}"))
                    for g in G2:
                        for b in G2:
                            r = HB[b]
                            pe.wait_ge(*a_gdn.sem_at(f"wT1{g}", i))
                            if b == 0 and g == 0:
                                pe.wait_ge(*v_gdn.sem_at("S311", i - 1))
                            else:
                                pe.wait_ge(*v_gdn.sem_at(f"S3{1 - b}{g if b else g - 1}", i))
                            heads(lambda h: mm(bank[g][3][r, h], wT[g][:, b, h], S[b][:, h])).then_inc(*p_gdn(f"W{b}{g}"))
                            pe.wait_ge(*v_gdn.sem_at(f"vn{b}{g}", i))
                            heads(lambda h: mm(bank[g][2][:, h], kd[g][r, h], vn[g][r, h])).then_inc(*p_gdn(f"dS{b}{g}"))

                            def read_out(h):
                                mm(bank[g][0][r, h], qdT[g][:, h, r], S[b][:, h], True, False)
                                return mm(bank[g][0][r, h], QKT[g][r, h], vn[g][r, h], False, True)
                            pe.wait_ge(*g_gdn.sem_at(f"qd{g}", i))
                            heads(read_out).then_inc(*p_gdn(f"o{b}{g}"))
                        pe.wait_ge(*v_gdn.sem_at(f"on{g}", i))
                        heads(lambda h: nc.tensor.transpose(bank[g][1][:, h], qn[g][:, h], ident[:])).then_inc(*p_gdn(f"ty{g}"))
        gdn.close()

        NG = w_group_router.shape[2]
        NE = w_expert_router.shape[2]
        NR = NG + NE
        FE = w_down.shape[2]
        hres = qkvT[:, 0:NT, :]
        xn_rows = nc.dram_tensor("xn_rows", (T, D), F32, kind="Internal").ap()
        route = ExitStack()
        logits = sb("logits", [P, NT, NR], ctx=route)
        gates = sb("gates", [P, NT, 2], ctx=route)
        mh1 = sb("mh1", [P, 1], ctx=route)
        eps1 = sb("eps1", [P, 1], ctx=route)

        a_out = Steps(sem("act_out"), both(["mhz", "mhc"]) + [f"{n}{g}" for g in G2 for n in ("sq", "xT0", "xT1")], credit=True)
        v_out = Steps(sem("dve_out"), both(["mlz", "mlc"]) + [f"{n}{g}" for g in G2 for n in ("h0", "h1", "xn")] + ["lg0", "lg1"], credit=True)
        g_out = Steps(sem("pool_out"), [f"{n}{g}" for g in G2 for n in ("ms", "rs")], credit=True)
        p_out = Steps(sem("pe_out"), both(["o"]) + [f"{n}{g}" for g in G2 for n in ("T", "r")], credit=True)
        s_wo = [sem(f"s_wo{s}") for s in range(2)]
        s_wo_hi, s_wo_lo = sem("s_wo_hi"), sem("s_wo_lo")
        s_wr, s_gb = sem("s_wr"), sem("s_gb")
        s_xr = [sem(f"s_xr{g}") for g in G2]
        s_xn = [sem(f"s_xn{g}") for g in G2]
        s_half = sem("s_half")
        s_sent = [sem(f"s_sent{g}") for g in G2]
        with ExitStack() as c5:
            wo = [sb(f"wo_{n}", [P, NJ, D], F32R, c5) for n in ("hi", "lo")]
            wo_raw = [sb(f"wo_raw{s}", [P, D], ctx=c5) for s in range(2)]
            mix = [[sb(f"mix_{n}{g}", [P, NJ, P], F32R, c5) for n in ("hi", "lo")] for g in G2]
            xr = [sb(f"xr{g}", [P, D], ctx=c5) for g in G2]
            xn2 = [sb(f"xn2{g}", [P, D], ctx=c5) for g in G2]
            xT = [sb(f"xT{g}", [P, NJ, P], ctx=c5) for g in G2]
            gB = sb("gB", [P, D], ctx=c5)
            wr = sb("wr", [P, NJ, NR], ctx=c5)
            junk5 = sb("junk5", [P, D], ctx=c5)
            s1 = [sb(f"s1{g}", [P, 1], ctx=c5) for g in G2]
            r1 = [sb(f"r1{g}", [P, 1], ctx=c5) for g in G2]
            ps_o = [psum(f"ps_o{g}", [P, 2, 512], ctx=c5) for g in G2]
            ps_T = [psum(f"ps_T{g}", [P, NJ, P], ctx=c5) for g in G2]
            ps_r = [t[:].rearrange("p j c -> p (j c)")[:, 0:NR] for t in ps_T]
            blk = c5.enter_context(nc.Block())
            parts = [(zT, 0, "z"), (convT, H, "c")]

            @blk.sync
            def _(sp):
                for j in range(NJ):
                    if j >= 2:
                        sp.wait_ge(s_wo_lo, j - 1)
                    sp.dma_start(wo_raw[j % 2][:], w_out[0, j * P:(j + 1) * P, :]).then_inc(s_wo[j % 2], 16)
                    if j == 1:
                        sp.dma_start(gB[:], g_moe.partition_broadcast(P)).then_inc(s_gb, 16)
                        sp.dma_start(wr[:, :, 0:NG], w_group_router[0].rearrange("(j p) n -> p j n", p=P)).then_inc(s_wr, 16)
                        sp.dma_start(wr[:, :, NG:NR], w_expert_router[0].rearrange("(j p) n -> p j n", p=P)).then_inc(s_wr, 16)
                for g in G2:
                    sp.sem_inc(s_sent[g], 1)
                with sp.Fori(0, NT // 2) as i:
                    for g in G2:
                        row = (2 * i + g) * P
                        sp.wait_ge(*v_out.sem_at(f"h1{g}", i - 1))
                        sp.dma_start(xr[g][:], x[0, ds(row, P), :]).then_inc(s_xr[g], 16)
                    for g in G2:
                        row = (2 * i + g) * P
                        sp.wait_ge(*v_out.sem_at(f"xn{g}", i))
                        sp.dma_start(xn_rows[ds(row, P), :], xn2[g][:]).then_inc(s_xn[g], 16)
                    for g in G2:
                        sp.wait_ge(s_xn[g], 16 + 16 * i)
                        sp.sem_inc(s_sent[g], 1)
                for g in G2:
                    sp.wait_ge(s_xn[g], 16 * NT // 2)

            @blk.scalar
            def _(act):
                for j in range(NJ):
                    act.wait_ge(s_wo[j % 2], 16 * (j // 2 + 1))
                    nc.scalar.activation(wo[0][:, j, :], wo_raw[j % 2][:], ACT.Copy).then_inc(s_wo_hi, 1)
                a_out.give_credit(act)
                with act.Fori(0, NT // 2) as i:
                    for src, m, n in parts:
                        for g in G2:
                            wait_alone(act, *p_out.sem_at(f"o{g}", i - 1))
                            nc.scalar.activation(mix[g][0][:, m:m + 4, :], src[:, :, ds((2 * i + g) * P, P)], ACT.Copy).then_inc(*a_out(f"mh{n}{g}"))
                    for g in G2:
                        wait_alone(act, *v_out.sem_at(f"h1{g}", i))
                        nc.scalar.activation(junk5[:].unsqueeze(1), hres[:, ds(2 * i + g, 1), :], ACT.Square, scale=float(D) ** -0.5, accum_out=s1[g][:]).then_inc(*a_out(f"sq{g}"))
                        act.wait_ge(*p_out.sem_at(f"T{g}", i))
                        act.wait_ge(*p_out.sem_at(f"r{g}", i - 1))
                        for h in range(2):
                            nc.scalar.activation(xT[g][:, 4 * h:4 * h + 4, :], ps_T[g][:, 4 * h:4 * h + 4, :], ACT.Copy).then_inc(*a_out(f"xT{h}{g}"))

            @blk.gpsimd
            def _(pool):
                nc.gpsimd.memset(mh1[:], -0.5).then_inc(s_half, 1)
                nc.gpsimd.memset(eps1[:], EPS).then_inc(s_half, 1)
                g_out.give_credit(pool)
                pool.wait_ge(s_half, 2)
                with pool.Fori(0, NT // 2) as i:
                    for g in G2:
                        pool.wait_ge(*a_out.sem_at(f"sq{g}", i))
                        nc.gpsimd.tensor_tensor(s1[g][:], s1[g][:], eps1[:], ALU.add).then_inc(*g_out(f"ms{g}"))
                        pool.wait_ge(*g_out.sem_at(f"ms{g}", i))
                        nc.gpsimd.tensor_tensor(r1[g][:], s1[g][:], mh1[:], ALU.pow).then_inc(*g_out(f"rs{g}"))

            @blk.vector
            def _(dve):
                for j in range(NJ):
                    dve.wait_ge(s_wo_hi, j + 1)
                    nc.vector.tensor_tensor(wo[1][:, j, :], wo_raw[j % 2][:], wo[0][:, j, :].bitcast(F32), ALU.subtract).then_inc(s_wo_lo, 1)
                v_out.give_credit(dve)
                dve.wait_ge(s_gb, 16)
                with dve.Fori(0, NT // 2) as i:
                    for src, m, n in parts:
                        for g in G2:
                            dve.wait_ge(*a_out.sem_at(f"mh{n}{g}", i))
                            nc.vector.tensor_tensor(mix[g][1][:, m:m + 4, :], src[:, :, ds((2 * i + g) * P, P)],
                                                    mix[g][0][:, m:m + 4, :].bitcast(F32), ALU.subtract).then_inc(*v_out(f"ml{n}{g}"))
                    for g in G2:
                        dve.wait_ge(*p_out.sem_at(f"o{g}", i))
                        dve.wait_ge(s_xr[g], 16 + 16 * i)
                        for h in range(2):
                            nc.vector.tensor_tensor(hres[:, ds(2 * i + g, 1), HF[h]], ps_o[g][:, h:h + 1, :], xr[g][:, HF[h]].unsqueeze(1),
                                                    ALU.add).then_inc(*v_out(f"h{h}{g}"))
                        dve.wait_ge(*g_out.sem_at(f"rs{g}", i))
                        dve.wait_ge(*p_out.sem_at(f"T{g}", i - 1))
                        dve.wait_ge(s_sent[g], i + 1)
                        nc.vector.scalar_tensor_tensor(xn2[g][:].unsqueeze(1), hres[:, ds(2 * i + g, 1), :], r1[g][:], gB[:].unsqueeze(1),
                                                       ALU.mult, ALU.mult).then_inc(*v_out(f"xn{g}"))
                    for g in G2:
                        dve.wait_ge(*p_out.sem_at(f"r{g}", i))
                        nc.vector.tensor_copy(logits[:, ds(2 * i + g, 1), :], ps_r[g].unsqueeze(1)).then_inc(*v_out(f"lg{g}"))

            @blk.tensor
            def _(pe):
                p_out.give_credit(pe)
                pe.wait_ge(s_wo_lo, NJ)
                pe.wait_ge(s_wr, 32)
                with pe.Fori(0, NT // 2) as i:
                    for g in G2:
                        pe.wait_ge(*v_out.sem_at(f"mlc{g}", i))
                        pe.wait_ge(*v_out.sem_at(f"h1{g}", i - 1))
                        for h in range(2):
                            for j in range(NJ):
                                last = mm3(ps_o[g][:, h, :], [mix[g][0][:, j, :], mix[g][1][:, j, :]],
                                           [wo[0][:, j, HF[h]], wo[1][:, j, HF[h]]], j == 0, j == NJ - 1)
                        last.then_inc(*p_out(f"o{g}"))
                    for g in G2:
                        pe.wait_ge(*v_out.sem_at(f"xn{g}", i))
                        pe.wait_ge(*v_out.sem_at(f"lg{g}", i - 1))
                        for j in range(NJ):
                            last = nc.tensor.transpose(ps_T[g][:, j, :], xn2[g][:, j * P:(j + 1) * P], ident[:])
                        last.then_inc(*p_out(f"T{g}"))
                        pe.wait_ge(*a_out.sem_at(f"xT1{g}", i))
                        for j in range(NJ):
                            last = nc.tensor.matmul(ps_r[g], xT[g][:, j, :], wr[:, j, :], start=j == 0, stop=j == NJ - 1)
                        last.then_inc(*p_out(f"r{g}"))

        C = 96
        MX = (T - 1) // C
        NOV = 2 * T // C
        NI = NE + NOV
        y_rows = nc.dram_tensor("y_rows", (NI * C, D), F32, kind="Internal").ap()
        gidx = sb("gidx", [C, NI], I32, route)
        ridx = sb("ridx", [P, NT, 2], I32, route)
        nov = sb("nov", [1, 1], I32, route)
        eov = sb("eov", [1, NOV], I32, route)
        s_zr, s_zsent = sem("s_zr"), sem("s_zsent")
        s_iota, s_rv, s_ra, s_rp = sem("s_iota"), sem("s_rv"), sem("s_ra"), sem("s_rp")
        W8 = [P, NT, NG]
        with ExitStack() as c6:
            i8 = sb("i8", [P, 8], ctx=c6)
            i64 = sb("i64", [P, NE], ctx=c6)
            iC = sb("iC", [P, C], ctx=c6)
            iN = sb("iN", [P, NI], ctx=c6)
            thr = sb("thr", [P, MX], ctx=c6)
            val = sb("val", [P, NT, 2], ctx=c6)
            stri = sb("stri", [P, P], BF16, c6)
            on16 = sb("on16", [P, P], BF16, c6)
            t8 = {n: sb("r8_" + n, W8, ctx=c6) for n in ("gd", "ge", "eq", "ca", "oh", "ing", "d", "e1", "c1", "o1", "d2", "e2", "c2")}
            t1 = {n: sb("r1_" + n, [P, NT, 1], ctx=c6) for n in ("gm", "gs", "gw", "gi", "m1", "i1", "m2", "i2", "ex", "dn", "rc")}
            t2 = {n: sb("r2_" + n, [P, NT, 2], ctx=c6) for n in ("ev", "rank", "m", "slot", "ovk", "a", "b", "c", "item", "mp", "row")}
            big = sb("r_big", [P, NT, NG, 8], ctx=c6)
            oh = sb("r_oh", [P, NT, 2, NE], BF16, c6)
            ohs = sb("r_ohs", [P, NT, NE], BF16, c6)
            tot = sb("r_tot", [P, NT, NE], ctx=c6)
            pre = sb("r_pre", [P, NT + 1, NE], ctx=c6)
            rt = sb("r_rt", [P, NT, NE], ctx=c6)
            w4 = sb("r_w4", [P, NT, 2, NE], ctx=c6)
            cm = sb("r_cm", [P, 2 * NT, MX], ctx=c6)
            cn = sb("r_cn", [P, NE, MX], ctx=c6)
            nex, cum, ovs, one64 = (sb("r_" + n, [P, NE], ctx=c6) for n in ("nex", "cum", "ovs", "one64"))
            itf = sb("r_itf", [P, 2 * NT, NI], ctx=c6)
            it16 = sb("r_it16", [P, 2 * NT, NI], F16, c6)
            sl16 = sb("r_sl16", [P, 2 * NT, C], F16, c6)
            tb, te = (sb("r_" + n, [C, NI], ctx=c6) for n in ("tb", "te"))
            ce = sb("r_ce", [1, NOV, NE], ctx=c6)
            zero = sb("zero", [C, D], ctx=c6)
            cf = sb("r_cf", [1, NOV], ctx=c6)
            ps_pre = psum("ps_pre", [P, NT, NE], ctx=c6)
            ps_tot = psum("ps_tot", [P, NT, NE], ctx=c6)
            ps_tab = psum("ps_tab", [P, 512], ctx=c6)
            blk = c6.enter_context(nc.Block())
            at = {}

            @blk.sync
            def _(sp):
                sp.wait_ge(s_zr, 1)
                for k in range(NOV):
                    sp.dma_start(y_rows[(NE + k) * C:(NE + k + 1) * C, :], zero[:]).then_inc(s_zsent, 16)
                sp.wait_ge(s_zsent, 16 * NOV)

            @blk.gpsimd
            def _(pool):
                nc.gpsimd.memset(zero[:], 0.0).then_inc(s_zr, 1)
                def iota(t, pattern, base, mult):
                    nc.gpsimd.iota(t[:], pattern, base=base, channel_multiplier=mult, allow_small_or_imprecise_dtypes=True).then_inc(s_iota, 1)
                iota(i8, [[1, 8]], 0, 0)
                iota(i64, [[1, NE]], 0, 0)
                iota(iC, [[1, C]], 0, 0)
                iota(iN, [[1, NI]], 0, 0)
                iota(thr, [[C, MX]], C, 0)
                iota(val, [[P, NT], [0, 2]], 1, 1)
                nc.gpsimd.memset(on16[:], 1.0).then_inc(s_iota, 1)
                nc.gpsimd.memset(stri[:], 1.0).then_inc(s_iota, 1)
                nc.gpsimd.memset(one64[:], 1.0).then_inc(s_iota, 1)
                nc.gpsimd.memset(pre[:, 0, :], 0.0).then_inc(s_iota, 1)
                pool.wait_ge(s_iota, 10)
                nc.gpsimd.affine_select(out=stri[:], in_=stri[:], compare_op=ALU.is_gt, fill=0.0, base=0,
                                        pattern=[[1, P]], channel_multiplier=-1).then_inc(s_iota, 1)

            @blk.vector
            def _(dve):
                done = 0

                def then(ins, name=None):
                    nonlocal done
                    done += 1
                    ins.then_inc(s_rv, 1)
                    dve.wait_ge(s_rv, done)
                    if name:
                        at[name] = done

                def tt(o, a, b, op, name=None):
                    then(nc.vector.tensor_tensor(o, a, b, op), name)

                def red(o, a, op):
                    then(nc.vector.tensor_reduce(o, a, axis=AX.X, op=op))

                def first(d, top_, eq, cand, idx, onehot):
                    tt(eq[:], d, top_.to_broadcast(W8), ALU.is_equal)
                    then(nc.vector.scalar_tensor_tensor(cand[:], eq[:], -100.0, i8[:].unsqueeze(1).to_broadcast(W8), ALU.mult, ALU.add))
                    red(idx[:], cand[:], ALU.min)
                    tt(onehot[:], cand[:], idx[:].to_broadcast(W8), ALU.is_equal)

                dve.wait_ge(s_iota, 11)
                lgG, lgE = logits[:, :, 0:NG], logits[:, :, NG:NR].rearrange("p t (g e) -> p t g e", g=NG)
                red(t1["gm"][:], lgG, ALU.max)
                tt(t8["gd"][:], lgG, t1["gm"][:].to_broadcast(W8), ALU.subtract, "gd")
                first(lgG, t1["gm"][:], t8["eq"], t8["ca"], t1["gi"], t8["oh"])
                tt(big[:], lgE, t8["oh"][:].unsqueeze(3).to_broadcast([P, NT, NG, 8]), ALU.mult)
                red(t8["ing"][:], big[:].rearrange("p t g e -> p t e g"), ALU.add)
                red(t1["m1"][:], t8["ing"][:], ALU.max)
                tt(t8["d"][:], t8["ing"][:], t1["m1"][:].to_broadcast(W8), ALU.subtract)
                first(t8["ing"][:], t1["m1"][:], t8["e1"], t8["c1"], t1["i1"], t8["o1"])
                then(nc.vector.scalar_tensor_tensor(t8["d2"][:], t8["o1"][:], NEG, t8["d"][:], ALU.mult, ALU.add))
                red(t1["m2"][:], t8["d2"][:], ALU.max)
                at["m2"] = done
                first(t8["d2"][:], t1["m2"][:], t8["e2"], t8["c2"], t1["i2"], t8["oh"])
                for k, i_k in enumerate(("i1", "i2")):
                    then(nc.vector.scalar_tensor_tensor(t2["ev"][:, :, k:k + 1], t1["gi"][:], 8.0, t1[i_k][:], ALU.mult, ALU.add))
                then(nc.vector.tensor_scalar(t2["ev"][:], t2["ev"][:], 900.0, None, ALU.add))
                full = [P, NT, 2, NE]
                for k in range(2):
                    tt(oh[:, :, k, :], i64[:].unsqueeze(1).to_broadcast([P, NT, NE]), t2["ev"][:, :, k:k + 1].to_broadcast([P, NT, NE]), ALU.is_equal)
                tt(ohs[:], oh[:, :, 0, :], oh[:, :, 1, :], ALU.add, "ohs")
                dve.wait_ge(s_ra, 2)
                red(t1["gs"][:], t8["ge"][:], ALU.add)
                then(nc.vector.reciprocal(t1["gw"][:], t1["gs"][:]))
                then(nc.vector.tensor_scalar(t1["dn"][:], t1["ex"][:], 1.0, None, ALU.add))
                then(nc.vector.reciprocal(t1["rc"][:], t1["dn"][:]))
                tt(gates[:, :, 0:1], t1["gw"][:], t1["rc"][:], ALU.mult)
                tt(gates[:, :, 1:2], gates[:, :, 0:1], t1["ex"][:], ALU.mult)
                dve.wait_ge(s_rp, 2)
                then(nc.vector.tensor_copy(tot[:], ps_tot[:]))
                for t in range(NT):
                    tt(pre[:, t + 1, :], pre[:, t, :], tot[:, t, :], ALU.add)
                tt(rt[:], ps_pre[:], pre[:, 0:NT, :], ALU.add)
                for k in range(2):
                    tt(w4[:, :, k, :], oh[:, :, k, :], rt[:], ALU.mult)
                red(t2["rank"][:], w4[:], ALU.add)
                rank = t2["rank"][:].rearrange("p t k -> p (t k)")
                tt(cm[:], rank.unsqueeze(2).to_broadcast([P, 2 * NT, MX]), thr[:].unsqueeze(1).to_broadcast([P, 2 * NT, MX]), ALU.is_ge)
                red(t2["m"][:].rearrange("p t k -> p (t k)"), cm[:], ALU.add)
                then(nc.vector.scalar_tensor_tensor(t2["slot"][:], t2["m"][:], -float(C), t2["rank"][:], ALU.mult, ALU.add))
                wide = [P, NE, MX]
                tt(cn[:], pre[:, NT, :].unsqueeze(2).to_broadcast(wide), thr[:].unsqueeze(1).to_broadcast(wide), ALU.is_gt)
                red(nex[:], cn[:], ALU.add)
                then(nc.vector.tensor_tensor_scan(cum[:], one64[:], nex[:], 0.0, ALU.mult, ALU.add))
                tt(ovs[:], cum[:], nex[:], ALU.subtract)
                for k in range(2):
                    tt(w4[:, :, k, :], oh[:, :, k, :], ovs[:].unsqueeze(1).to_broadcast([P, NT, NE]), ALU.mult)
                red(t2["ovk"][:], w4[:], ALU.add)
                tt(t2["a"][:], t2["ovk"][:], t2["m"][:], ALU.add)
                tt(t2["b"][:], t2["a"][:], t2["ev"][:], ALU.subtract)
                then(nc.vector.tensor_scalar(t2["mp"][:], t2["m"][:], 0.5, None, ALU.is_ge))
                then(nc.vector.scalar_tensor_tensor(t2["c"][:], t2["b"][:], float(NE - 1), t2["mp"][:], ALU.add, ALU.mult))
                tt(t2["item"][:], t2["c"][:], t2["ev"][:], ALU.add)
                then(nc.vector.scalar_tensor_tensor(t2["row"][:], t2["item"][:], float(C), t2["slot"][:], ALU.mult, ALU.add))
                then(nc.vector.tensor_copy(ridx[:], t2["row"][:]))
                item = t2["item"][:].rearrange("p t k -> p (t k)")
                wn = [P, 2 * NT, NI]
                tt(itf[:], iN[:].unsqueeze(1).to_broadcast(wn), item.unsqueeze(2).to_broadcast(wn), ALU.is_equal)
                tt(it16[:], itf[:], val[:].rearrange("p t k -> p (t k)").unsqueeze(2).to_broadcast(wn), ALU.mult)
                wc = [P, 2 * NT, C]
                tt(sl16[:], iC[:].unsqueeze(1).to_broadcast(wc), t2["slot"][:].rearrange("p t k -> p (t k)").unsqueeze(2).to_broadcast(wc),
                   ALU.is_equal, "onehots")
                then(nc.vector.tensor_copy(nov[:], cum[0:1, NE - 1:NE]))
                wo_ = [1, NOV, NE]
                tt(ce[:], iN[0:1, 0:NOV].unsqueeze(2).to_broadcast(wo_), cum[0:1, :].unsqueeze(1).to_broadcast(wo_), ALU.is_ge)
                red(cf[:], ce[:], ALU.add)
                then(nc.vector.tensor_scalar(eov[:], cf[:], float(NE - 1), None, ALU.min))
                dve.wait_ge(s_rp, 3)
                then(nc.vector.tensor_copy(tb[:], ps_tab[0:C, 0:NI]))
                then(nc.vector.tensor_scalar(te[:], tb[:], 0.5, 4.0 * T, ALU.is_lt, ALU.mult))
                tt(te[:], te[:], tb[:], ALU.add)
                then(nc.vector.tensor_scalar(te[:], te[:], -1.0, None, ALU.add))
                then(nc.vector.tensor_copy(gidx[:], te[:]))

            @blk.scalar
            def _(act):
                act.wait_ge(s_rv, at["gd"])
                nc.scalar.activation(t8["ge"][:], t8["gd"][:], ACT.Exp).then_inc(s_ra, 1)
                act.wait_ge(s_rv, at["m2"])
                nc.scalar.activation(t1["ex"][:], t1["m2"][:], ACT.Exp).then_inc(s_ra, 1)

            @blk.tensor
            def _(pe):
                pe.wait_ge(s_iota, 11)
                pe.wait_ge(s_rv, at["ohs"])
                flat = ohs[:].rearrange("p t e -> p (t e)")
                nc.tensor.matmul(ps_pre[:].rearrange("p t e -> p (t e)"), stri[:], flat, start=True, stop=True).then_inc(s_rp, 1)
                nc.tensor.matmul(ps_tot[:].rearrange("p t e -> p (t e)"), on16[:], flat, start=True, stop=True).then_inc(s_rp, 1)
                pe.wait_ge(s_rv, at["onehots"])
                for n in range(2 * NT):
                    last = nc.tensor.matmul(ps_tab[0:C, 0:NI], sl16[:, n, :], it16[:, n, :], start=n == 0, stop=n == 2 * NT - 1)
                last.then_inc(s_rp, 1)

        NQX = 4
        NJF = FE // P
        s_up = [sem(f"s_up{q}") for q in range(NQX)]
        s_dn = [sem(f"s_dn{q}") for q in range(NQX)]
        s_idx = sem("s_idx")
        s_gat = [sem(f"s_gat{q}") for q in range(NQX)]
        s_sto = [sem(f"s_sto{s}") for s in range(2)]
        s_clear = sem("s_clear")
        s_T, s_xt, s_u, s_sil, s_h, s_d, s_y0, s_y1 = (sem("moe_" + n) for n in ("T", "xt", "u", "sil", "h", "d", "y0", "y1"))
        with ExitStack() as c7:
            wup = [sb(f"wup{q}", [P, NJ, 2 * FE], ctx=c7) for q in range(NQX)]
            wdn = [zT[:, 0:NJF, :], zT[:, NJF:2 * NJF, :], convT[:, 0:NJF, :], convT[:, NJF:2 * NJF, :]]
            gi = [sb(f"gi{q}", [C, 1], I32, c7) for q in range(NQX)]
            xg = [sb(f"xg{q}", [C, D], ctx=c7) for q in range(NQX)]
            xgT = [sb(f"xgT{s}", [P, NJ, C], ctx=c7) for s in range(2)]
            sil = [sb(f"sil{s}", [P, NJF, C], ctx=c7) for s in range(2)]
            hT = [sb(f"hT{s}", [P, NJF, C], ctx=c7) for s in range(2)]
            ye = [sb(f"ye{s}", [C, D], ctx=c7) for s in range(2)]
            ps_x = [psum(f"ps_xg{h}", [P, 512], ctx=c7) for h in range(2)]
            ps_u = [psum(f"ps_u{s}", [P, 512], ctx=c7) for s in range(2)]
            ps_y = [psum(f"ps_y{s}", [P, 2, 512], ctx=c7) for s in range(2)]
            blk = c7.enter_context(nc.Block())
            up_p = w_up[0].rearrange("e (p j) n -> p e j n", j=NJ)
            dn_p = w_down[0].rearrange("e (p j) n -> p e j n", j=NJF)
            HJ = NJ // 2

            def half_x(h):
                return ps_x[h][:, 0:HJ * C].rearrange("p (j c) -> p j c", j=HJ)

            def quarter(s):
                return ps_u[s][:, 0:2 * NJF * C].rearrange("p (m c) -> p m c", c=C)

            def fetch_weights(sp, q, e):
                sp.dma_start(wup[q][:], up_p[:, e, :, :]).then_inc(s_up[q], 16)
                sp.dma_start(wdn[q], dn_p[:, e, :, :]).then_inc(s_dn[q], 16)

            def fetch_tokens(pool, q, item, count):
                nc.gpsimd.tensor_copy(gi[q][:], gidx[:, item]).then_inc(s_idx, 1)
                wait_alone(pool, s_idx, count)
                nc.gpsimd.indirect_dma_start(xg[q][:], None, xn_rows, bass.IndirectOffsetOnAxis(gi[q][:, 0:1], 0),
                                             bounds_check=T - 1, oob_is_err=False).then_inc(s_gat[q], 16)

            def store_results(sp, s, row):
                sp.dma_start(y_rows[ds(row, C), :], ye[s][:]).then_inc(s_sto[s], 16)

            def transpose_tokens(q):
                for j in range(NJ):
                    last = nc.tensor.transpose(half_x(j // HJ)[:, j % HJ, :], xg[q][:, j:D:NJ], ident[0:C, 0:C])
                last.then_inc(s_T, 1)

            def up(s, q):
                for m in range(2 * NJF):
                    first_col = m // NJF * FE + m % NJF
                    for j in range(NJ):
                        last = nc.tensor.matmul(quarter(s)[:, m, :], wup[q][:, j, first_col:first_col + NJF * P - NJF + 1:NJF],
                                                xgT[s][:, j, :], start=j == 0, stop=j == NJ - 1)
                last.then_inc(s_u, 1)

            def down(s, q):
                for h in range(2):
                    for f in range(NJF):
                        last = nc.tensor.matmul(ps_y[s][0:C, h, :], hT[s][:, f, :], wdn[q][:, f, HF[h]], start=f == 0, stop=f == NJF - 1)
                last.then_inc(s_d, 1)

            NQ4 = NE // NQX

            @blk.sync
            def _(sp):
                for q in range(NQX):
                    fetch_weights(sp, q, q)
                with sp.Fori(0, NQ4 - 1) as i:
                    for q in range(NQX):
                        e = NQX * i + q
                        wait_alone(sp, s_d, e + 1)
                        fetch_weights(sp, q, ds(e + NQX, 1))
                        wait_alone(sp, s_y0, e + 1)
                        wait_alone(sp, s_y1, e + 1)
                        store_results(sp, q % 2, e * C)
                for q in range(NQX):
                    e = NE - NQX + q
                    wait_alone(sp, s_y0, e + 1)
                    wait_alone(sp, s_y1, e + 1)
                    store_results(sp, q % 2, e * C)
                n_over = sp.value_load(nov[0:1, 0:1], min_val=0, max_val=NOV)
                with sp.If(n_over > 0):
                    with sp.Fori(0, n_over) as k:
                        wait_alone(sp, s_d, NE + k)
                        e = sp.value_load(eov[0:1, ds(k, 1)], min_val=0, max_val=NE - 1)
                        fetch_weights(sp, 0, ds(e, 1))
                        wait_alone(sp, s_y0, NE + 1 + k)
                        wait_alone(sp, s_y1, NE + 1 + k)
                        store_results(sp, 0, (NE + k) * C)
                        wait_alone(sp, s_sto[0], 16 * NE // 2 + 16 * k + 16)
                for s in range(2):
                    sp.wait_ge(s_sto[s], 16 * NE // 2)

            @blk.gpsimd
            def _(pool):
                pool.wait_ge(s_clear, 1)
                for q in range(NQX):
                    fetch_tokens(pool, q, slice(q, q + 1), q + 1)
                with pool.Fori(1, NQ4) as i:
                    for q in range(NQX):
                        e = NQX * i + q
                        wait_alone(pool, s_T, e - NQX + 1)
                        fetch_tokens(pool, q, ds(e, 1), e + 1)
                n_over = pool.value_load(nov[0:1, 0:1], min_val=0, max_val=NOV)
                with pool.If(n_over > 0):
                    with pool.Fori(0, n_over) as k:
                        wait_alone(pool, s_T, NE + k)
                        fetch_tokens(pool, 0, ds(NE + k, 1), NE + 1 + k)

            @blk.scalar
            def _(act):
                def tokens(s, e):
                    act.wait_ge(s_T, e + 1)
                    nc.scalar.activation(xgT[s][:, 0:HJ, :], half_x(0), ACT.Copy)
                    nc.scalar.activation(xgT[s][:, HJ:NJ, :], half_x(1), ACT.Copy).then_inc(s_xt, 1)

                def silu(s, e):
                    act.wait_ge(s_u, e + 1)
                    nc.scalar.activation(sil[s][:], quarter(s)[:, 0:NJF, :], ACT.Silu).then_inc(s_sil, 1)

                def result(s, e, free):
                    act.wait_ge(s_d, e + 1)
                    if free is not None:
                        act.wait_ge(s_sto[s], free)
                    nc.scalar.activation(ye[s][:, HF[0]], ps_y[s][0:C, 0, :], ACT.Copy).then_inc(s_y0, 1)

                tokens(0, 0)

                def item(i, q, last=False):
                    e, s = NQX * i + q, q % 2
                    silu(s, e)
                    if not last:
                        tokens(1 - s, e + 1)
                    free = 16 * (2 * i + q // 2)
                    result(s, e, None if isinstance(free, int) and free == 0 else free)

                for q in range(NQX):
                    item(0, q)
                with act.Fori(1, NQ4 - 1) as i:
                    for q in range(NQX):
                        item(i, q)
                for q in range(NQX):
                    item(NQ4 - 1, q, q == NQX - 1)
                n_over = act.value_load(nov[0:1, 0:1], min_val=0, max_val=NOV)
                with act.If(n_over > 0):
                    with act.Fori(0, n_over) as k:
                        tokens(0, NE + k)
                        silu(0, NE + k)
                        result(0, NE + k, 16 * NE // 2 + 16 * k)

            @blk.vector
            def _(dve):
                for q in range(NQX):
                    last = nc.vector.memset(xg[q][:], 0.0)
                last.then_inc(s_clear, 1)

                def item(i, q):
                    e, s = NQX * i + q, q % 2
                    finish(s, e, 16 * (2 * i + q // 2))

                def finish(s, e, free):
                    dve.wait_ge(s_sil, e + 1)
                    nc.vector.tensor_tensor(hT[s][:], sil[s][:], quarter(s)[:, NJF:2 * NJF, :], ALU.mult).then_inc(s_h, 1)
                    dve.wait_ge(s_d, e + 1)
                    if not (isinstance(free, int) and free == 0):
                        dve.wait_ge(s_sto[s], free)
                    nc.vector.tensor_copy(ye[s][:, HF[1]], ps_y[s][0:C, 1, :]).then_inc(s_y1, 1)

                for q in range(NQX):
                    item(0, q)
                with dve.Fori(1, NQ4) as i:
                    for q in range(NQX):
                        item(i, q)
                n_over = dve.value_load(nov[0:1, 0:1], min_val=0, max_val=NOV)
                with dve.If(n_over > 0):
                    with dve.Fori(0, n_over) as k:
                        finish(0, NE + k, 16 * NE // 2 + 16 * k)

            @blk.tensor
            def _(pe):
                def tokens(q, e, landed):
                    pe.wait_ge(s_gat[q], landed)
                    if not (isinstance(e, int) and e == 0):
                        pe.wait_ge(s_xt, e)
                    transpose_tokens(q)

                def item(i, q, last=False):
                    e, s = NQX * i + q, q % 2
                    if not last:
                        n = (q + 1) % NQX
                        turn = 16 * (i + 1 if q + 1 < NQX else i + 2)
                        tokens(n, e + 1, turn)
                        pe.wait_ge(s_xt, e + 2)
                        pe.wait_ge(s_up[n], turn)
                        if not (isinstance(e, int) and e == 0):
                            pe.wait_ge(s_h, e)
                        up(1 - s, n)
                    pe.wait_ge(s_h, e + 1)
                    pe.wait_ge(s_dn[q], 16 * (i + 1))
                    if not (isinstance(e, int) and e < 2):
                        pe.wait_ge(s_y0, e - 1)
                        pe.wait_ge(s_y1, e - 1)
                    down(s, q)

                tokens(0, 0, 16)
                pe.wait_ge(s_xt, 1)
                pe.wait_ge(s_up[0], 16)
                up(0, 0)
                for q in range(NQX):
                    item(0, q)
                with pe.Fori(1, NQ4 - 1) as i:
                    for q in range(NQX):
                        item(i, q)
                for q in range(NQX):
                    item(NQ4 - 1, q, q == NQX - 1)
                n_over = pe.value_load(nov[0:1, 0:1], min_val=0, max_val=NOV)
                with pe.If(n_over > 0):
                    with pe.Fori(0, n_over) as k:
                        tokens(0, NE + k, 16 * NQ4 + 16 * k + 16)
                        pe.wait_ge(s_xt, NE + 1 + k)
                        pe.wait_ge(s_up[0], 16 * NQ4 + 16 + 16 * k)
                        up(0, 0)
                        pe.wait_ge(s_h, NE + 1 + k)
                        pe.wait_ge(s_dn[0], 16 * NQ4 + 16 + 16 * k)
                        down(0, 0)

        PD = p.shape[3]
        NJP = PD // P
        a_fin = Steps(sem("act_fin"), [f"{n}{g}" for g in G2 for n in ("sqa", "hi", "phi", "sg0", "sg1", "sqb")], credit=True)
        v_fin = Steps(sem("dve_fin"), [f"{n}{g}" for g in G2 for n in ("y1", "y2", "hn", "plo", "lo", "m0", "m1", "h3", "out")], credit=True)
        g_fin = Steps(sem("pool_fin"), [f"{n}{g}" for g in G2 for n in ("msa", "rsa", "msb", "rsb")], credit=True)
        p_fin = Steps(sem("pe_fin"), [f"{n}{g}" for g in G2 for n in ("pT", "hT", "pp", "gate")], credit=True)
        s_wg = [sem(f"s_wg{s}") for s in range(2)]
        s_wg_hi, s_wg_lo = sem("s_wg_hi"), sem("s_wg_lo")
        s_gfin, s_fi = sem("s_gfin"), sem("s_fi")
        s_fsent = [sem(f"s_fsent{g}") for g in G2]
        s_fy = [sem(f"s_fy{g}") for g in G2]
        s_fz = [sem(f"s_fz{g}") for g in G2]
        s_fp = [sem(f"s_fp{g}") for g in G2]
        s_fo = [sem(f"s_fo{g}") for g in G2]
        with ExitStack() as c8:
            NWJ = NJ + NJP
            wg = [sb(f"wg_{n}", [P, NWJ, D], F32R, c8) for n in ("hi", "lo")]
            wg_raw = [zT[:, 0, :], zT[:, 1, :]]
            yy = [convT[:, g, :] for g in G2]
            yz = [convT[:, 2 + g, :] for g in G2]
            pin = [sb(f"pin{g}", [P, PD], ctx=c8) for g in G2]
            hn = [qkvT[:, NT + g, :] for g in G2]
            ho = [qkvT[:, NT + 2 + g, :] for g in G2]
            hx = [[sb(f"hx_{n}{g}", [P, NJ, P], F32R, c8) for n in ("hi", "lo")] for g in G2]
            px = [[sb(f"px_{n}{g}", [P, NJP, P], F32R, c8) for n in ("hi", "lo")] for g in G2]
            gP = zT[:, 2, :]
            gF = zT[:, 3, :]
            junk8 = sb("junk8", [P, D], ctx=c8)
            fi = [[sb(f"fi{g}{k}", [P, 1], I32, c8) for k in range(2)] for g in G2]
            s8 = [sb(f"s8{g}", [P, 1], ctx=c8) for g in G2]
            r8 = [sb(f"r8{g}", [P, 1], ctx=c8) for g in G2]
            ps_g = psum("ps_gate", [P, 2, 512], ctx=c8)
            ps_p = psum("ps_pp", [P, 2, 512], ctx=c8)
            ps_h = psum("ps_hT", [P, NJ, P], ctx=c8)
            ps_q = psum("ps_pT", [P, 512], ctx=c8)
            blk = c8.enter_context(nc.Block())
            pq = ps_q[:, 0:PD].rearrange("p (j c) -> p j c", j=NJP)

            def wrow(j):
                return w_ple_gate[0, j * P:(j + 1) * P, :] if j < NJ else w_ple_proj[0, (j - NJ) * P:(j - NJ + 1) * P, :]

            @blk.sync
            def _(sp):
                sp.dma_start(gP, g_ple.partition_broadcast(P)).then_inc(s_gfin, 16)
                sp.dma_start(gF, g_final.unsqueeze(0).partition_broadcast(P)).then_inc(s_gfin, 16)
                for j in range(NWJ):
                    if j >= 2:
                        sp.wait_ge(s_wg_lo, j - 1)
                    sp.dma_start(wg_raw[j % 2], wrow(j)).then_inc(s_wg[j % 2], 16)
                for g in G2:
                    sp.sem_inc(s_fsent[g], 1)
                with sp.Fori(0, NT // 2) as i:
                    for g in G2:
                        row = (2 * i + g) * P
                        sp.wait_ge(*v_fin.sem_at(f"m1{g}", i - 1))
                        sp.dma_start(pin[g][:], p[0, 0, ds(row, P), :]).then_inc(s_fp[g], 16)
                    for g in G2:
                        row = (2 * i + g) * P
                        sp.wait_ge(*v_fin.sem_at(f"out{g}", i))
                        sp.dma_start(out[0, ds(row, P), :], ho[g]).then_inc(s_fo[g], 16)
                    for g in G2:
                        sp.wait_ge(s_fo[g], 16 + 16 * i)
                        sp.sem_inc(s_fsent[g], 1)
                for g in G2:
                    sp.wait_ge(s_fo[g], 16 * NT // 2)

            @blk.scalar
            def _(act):
                for j in range(NWJ):
                    act.wait_ge(s_wg[j % 2], 16 * (j // 2 + 1))
                    nc.scalar.activation(wg[0][:, j, :], wg_raw[j % 2], ACT.Copy).then_inc(s_wg_hi, 1)
                a_fin.give_credit(act)
                with act.Fori(0, NT // 2) as i:
                    for g in G2:
                        hg = hres[:, ds(2 * i + g, 1), :]
                        act.wait_ge(*v_fin.sem_at(f"y2{g}", i))
                        wait_alone(act, *(a_fin.sem_at("sqb1", i - 1) if g == 0 else a_fin.sem_at("sqb0", i)))
                        nc.scalar.activation(junk8[:].unsqueeze(1), hg, ACT.Square, scale=float(D) ** -0.5, accum_out=s8[g][:]).then_inc(*a_fin(f"sqa{g}"))
                        act.wait_ge(*p_fin.sem_at(f"hT{g}", i))
                        act.wait_ge(*p_fin.sem_at(f"gate{g}", i - 1))
                        nc.scalar.activation(hx[g][0][:], ps_h[:], ACT.Copy).then_inc(*a_fin(f"hi{g}"))
                        nc.scalar.activation(px[g][0][:], pq, ACT.Copy).then_inc(*a_fin(f"phi{g}"))
                        act.wait_ge(*p_fin.sem_at(f"gate{g}", i))
                        for h in range(2):
                            nc.scalar.activation(hn[g][:, HF[h]], ps_g[:, h, :], ACT.Sigmoid).then_inc(*a_fin(f"sg{h}{g}"))
                        wait_alone(act, *v_fin.sem_at(f"h3{g}", i))
                        nc.scalar.activation(junk8[:].unsqueeze(1), hg, ACT.Square, scale=float(D) ** -0.5, accum_out=s8[g][:]).then_inc(*a_fin(f"sqb{g}"))

            @blk.gpsimd
            def _(pool):
                g_fin.give_credit(pool)
                with pool.Fori(0, NT // 2) as i:
                    for g in G2:
                        for k, (y, landed) in enumerate(((yy[g], s_fy[g]), (yz[g], s_fz[g]))):
                            wait_alone(pool, *v_fin.sem_at(f"m1{g}", i - 1))
                            nc.gpsimd.tensor_copy(fi[g][k][:], ridx[:, ds(2 * i + g, 1), k:k + 1].squeeze(1)).then_inc(s_fi, 1)
                            wait_alone(pool, s_fi, 4 * i + 2 * g + k + 1)
                            nc.gpsimd.indirect_dma_start(y, None, y_rows, bass.IndirectOffsetOnAxis(fi[g][k][:, 0:1], 0),
                                                         bounds_check=NI * C - 1, oob_is_err=False).then_inc(landed, 16)
                    for g in G2:
                        for n in "ab":
                            pool.wait_ge(*a_fin.sem_at(f"sq{n}{g}", i))
                            nc.gpsimd.tensor_tensor(s8[g][:], s8[g][:], eps1[:], ALU.add).then_inc(*g_fin(f"ms{n}{g}"))
                            pool.wait_ge(*g_fin.sem_at(f"ms{n}{g}", i))
                            nc.gpsimd.tensor_tensor(r8[g][:], s8[g][:], mh1[:], ALU.pow).then_inc(*g_fin(f"rs{n}{g}"))

            @blk.vector
            def _(dve):
                for j in range(NWJ):
                    dve.wait_ge(s_wg_hi, j + 1)
                    nc.vector.tensor_tensor(wg[1][:, j, :], wg_raw[j % 2], wg[0][:, j, :].bitcast(F32), ALU.subtract).then_inc(s_wg_lo, 1)
                v_fin.give_credit(dve)
                dve.wait_ge(s_gfin, 32)
                with dve.Fori(0, NT // 2) as i:
                    for g in G2:
                        t = 2 * i + g
                        hg = hres[:, ds(t, 1), :]

                        def gate(k):
                            return gates[:, ds(t, 1), k:k + 1].squeeze(1)
                        dve.wait_ge(s_fy[g], 16 + 16 * i)
                        nc.vector.scalar_tensor_tensor(hg, yy[g].unsqueeze(1), gate(0), hg, ALU.mult, ALU.add).then_inc(*v_fin(f"y1{g}"))
                        dve.wait_ge(s_fz[g], 16 + 16 * i)
                        dve.wait_ge(*v_fin.sem_at(f"y1{g}", i))
                        nc.vector.scalar_tensor_tensor(hg, yz[g].unsqueeze(1), gate(1), hg, ALU.mult, ALU.add).then_inc(*v_fin(f"y2{g}"))
                        dve.wait_ge(*g_fin.sem_at(f"rsa{g}", i))
                        nc.vector.scalar_tensor_tensor(hn[g].unsqueeze(1), hg, r8[g][:], gP.unsqueeze(1), ALU.mult, ALU.mult).then_inc(*v_fin(f"hn{g}"))
                        dve.wait_ge(*a_fin.sem_at(f"phi{g}", i))
                        nc.vector.tensor_tensor(px[g][1][:], pq, px[g][0][:].bitcast(F32), ALU.subtract).then_inc(*v_fin(f"plo{g}"))
                        nc.vector.tensor_tensor(hx[g][1][:], ps_h[:], hx[g][0][:].bitcast(F32), ALU.subtract).then_inc(*v_fin(f"lo{g}"))
                        for h in range(2):
                            dve.wait_ge(*p_fin.sem_at(f"pp{g}", i))
                            dve.wait_ge(*a_fin.sem_at(f"sg{h}{g}", i))
                            nc.vector.tensor_tensor(yy[g][:, HF[h]], hn[g][:, HF[h]], ps_p[:, h, :], ALU.mult).then_inc(*v_fin(f"m{h}{g}"))
                        dve.wait_ge(*v_fin.sem_at(f"m1{g}", i))
                        nc.vector.tensor_tensor(hg, hg, yy[g].unsqueeze(1), ALU.add).then_inc(*v_fin(f"h3{g}"))
                        dve.wait_ge(*g_fin.sem_at(f"rsb{g}", i))
                        dve.wait_ge(s_fsent[g], i + 1)
                        nc.vector.scalar_tensor_tensor(ho[g].unsqueeze(1), hg, r8[g][:], gF.unsqueeze(1), ALU.mult, ALU.mult).then_inc(*v_fin(f"out{g}"))

            @blk.tensor
            def _(pe):
                p_fin.give_credit(pe)
                pe.wait_ge(s_wg_lo, NWJ)
                with pe.Fori(0, NT // 2) as i:
                    for g in G2:
                        pe.wait_ge(s_fp[g], 16 + 16 * i)
                        pe.wait_ge(*(v_fin.sem_at("m11", i - 1) if g == 0 else v_fin.sem_at("m10", i)))
                        for j in range(NJP):
                            last = nc.tensor.transpose(pq[:, j, :], pin[g][:, j * P:(j + 1) * P], ident[:])
                        last.then_inc(*p_fin(f"pT{g}"))
                        pe.wait_ge(*v_fin.sem_at(f"hn{g}", i))
                        for j in range(NJ):
                            last = nc.tensor.transpose(ps_h[:, j, :], hn[g][:, j * P:(j + 1) * P], ident[:])
                        last.then_inc(*p_fin(f"hT{g}"))
                        pe.wait_ge(*v_fin.sem_at(f"plo{g}", i))
                        for h in range(2):
                            for j in range(NJP):
                                last = mm3(ps_p[:, h, :], [px[g][0][:, j, :], px[g][1][:, j, :]],
                                           [wg[0][:, NJ + j, HF[h]], wg[1][:, NJ + j, HF[h]]], j == 0, j == NJP - 1)
                        last.then_inc(*p_fin(f"pp{g}"))
                        pe.wait_ge(*v_fin.sem_at(f"lo{g}", i))
                        for h in range(2):
                            for j in range(NJ):
                                last = mm3(ps_g[:, h, :], [hx[g][0][:, j, :], hx[g][1][:, j, :]],
                                           [wg[0][:, j, HF[h]], wg[1][:, j, HF[h]]], j == 0, j == NJ - 1)
                        last.then_inc(*p_fin(f"gate{g}"))
        route.close()
        proj.close()


INS = ["x", "p", "g_mix", "w_in", "w_conv_qkv", "a_log", "dt_bias", "g_gdn_out", "b_glu", "w_conv_dw",
       "b_conv_dw", "ln_conv_g", "ln_conv_b", "w_out", "g_moe", "w_group_router", "w_expert_router",
       "w_up", "w_down", "g_ple", "w_ple_gate", "w_ple_proj", "g_final"]


def kernel(**inputs):
    import numpy as _np
    import concourse.bacc as _bacc
    from concourse import mybir as _mybir
    from concourse.bass_utils import run_bass_kernel_spmd as _run

    nc = _bacc.Bacc("TRN2", target_bir_lowering=False, num_devices=1)
    arrays, args = {}, []
    for name in INS:
        a = _np.ascontiguousarray(inputs[name])
        arrays[f"in_{name}_dram"] = a
        args.append(nc.dram_tensor(f"in_{name}_dram", a.shape, _mybir.dt.from_np(a.dtype), kind="ExternalInput").ap())
    shape = tuple(inputs["x"].shape)
    out = nc.dram_tensor("out_dram", shape, _mybir.dt.float32, kind="ExternalOutput").ap()
    hybrid_block_kernel(nc, *args, out)
    r = _run(nc, [arrays], core_ids=[0])
    return r.results[0]["out_dram"]
```
